# Optimizing a Trainium2 kernel written in Bass

```python
import jax, jax.numpy as jnp
from jax import lax
import numpy as np
import math
import jax
import jax.numpy as jnp

D_MODEL = 1024
BATCH = 1
SEQ = 512
DEPTH = 2

GRID_W = 64
CTX_LEN = 256
N_MIXERS = 2
GQA_HEADS = 16
GQA_KV_HEADS = 4
GQA_GROUP = GQA_HEADS // GQA_KV_HEADS
GQA_HEAD_DIM = D_MODEL // GQA_HEADS
MLA_HEADS = 16
MLA_Q_RANK = (3 * D_MODEL) // 8
MLA_KV_RANK = D_MODEL // 4
MLA_NOPE_DIM = 64
MLA_ROPE_DIM = 32
MLA_V_DIM = 64
FFN_HIDDEN = 4 * D_MODEL
ROPE_THETA = 10000.0
Q_BLOCK = 128
NORM_EPS = 1e-6
DEEPNORM_ALPHA = (2.0 * DEPTH) ** 0.25
DEEPNORM_BETA = (8.0 * DEPTH) ** -0.25


def layer_norm(x, g, b):
    xf = x.astype(jnp.float32)
    mu = jnp.mean(xf, axis=-1, keepdims=True)
    var = jnp.mean(jnp.square(xf - mu), axis=-1, keepdims=True)
    return ((xf - mu) * lax.rsqrt(var + NORM_EPS) * g.astype(jnp.float32) + b.astype(jnp.float32)).astype(x.dtype)

def rms_norm(x, g):
    xf = x.astype(jnp.float32)
    ms = jnp.mean(jnp.square(xf), axis=-1, keepdims=True)
    return (xf * lax.rsqrt(ms + NORM_EPS) * g.astype(jnp.float32)).astype(x.dtype)

def grid_rope_tables(n_tok, rot_dim):
    rows = n_tok // GRID_W
    row = jnp.broadcast_to(jnp.arange(rows, dtype=jnp.float32)[:, None], (rows, GRID_W)).reshape(-1)
    col = jnp.broadcast_to(jnp.arange(GRID_W, dtype=jnp.float32)[None, :], (rows, GRID_W)).reshape(-1)
    axis_dim = rot_dim // 2
    inv_freq = ROPE_THETA ** (-jnp.arange(0, axis_dim, 2, dtype=jnp.float32) / axis_dim)
    ang_row = row[:, None] * inv_freq[None, :]
    ang_col = col[:, None] * inv_freq[None, :]
    return (jnp.cos(ang_row), jnp.sin(ang_row), jnp.cos(ang_col), jnp.sin(ang_col))

def rotate_axis(x, cos, sin):
    x1, x2 = jnp.split(x, 2, axis=-1)
    c = cos[:, None, :]
    s = sin[:, None, :]
    return jnp.concatenate([x1 * c - x2 * s, x2 * c + x1 * s], axis=-1)

def apply_grid_rope(x, tables):
    cr, sr, cc, sc = tables
    half = x.shape[-1] // 2
    xf = x.astype(jnp.float32)
    out = jnp.concatenate([rotate_axis(xf[..., :half], cr, sr), rotate_axis(xf[..., half:], cc, sc)], axis=-1)
    return out.astype(x.dtype)

def block_attention(q, k, v):
    b, sq, kvh, g, dk = q.shape
    nb = sq // Q_BLOCK
    scale = dk ** -0.5
    qb = jnp.moveaxis(q.reshape(b, nb, Q_BLOCK, kvh, g, dk), 1, 0)

    def one_block(qi):
        s = jnp.einsum('bqhgd,bkhd->bhgqk', qi, k, preferred_element_type=jnp.float32) * scale
        p = jax.nn.softmax(s, axis=-1).astype(v.dtype)
        return jnp.einsum('bhgqk,bkhe->bqhge', p, v)

    o = lax.map(one_block, qb)
    return jnp.moveaxis(o, 0, 1).reshape(b, sq, kvh * g * v.shape[-1])

def gqa_mixer(h_lat, h_ctx, w_qkv, q_norm, k_norm, w_o, rope, need_ctx):
    def project(h, rotate):
        b, n, _ = h.shape
        q, k, v = jnp.split(h @ w_qkv, [GQA_HEADS * GQA_HEAD_DIM, (GQA_HEADS + GQA_KV_HEADS) * GQA_HEAD_DIM], axis=-1)
        q = rms_norm(q.reshape(b, n, GQA_HEADS, GQA_HEAD_DIM), q_norm)
        k = rms_norm(k.reshape(b, n, GQA_KV_HEADS, GQA_HEAD_DIM), k_norm)
        v = v.reshape(b, n, GQA_KV_HEADS, GQA_HEAD_DIM)
        if rotate:
            q = apply_grid_rope(q, rope)
            k = apply_grid_rope(k, rope)
        return q.reshape(b, n, GQA_KV_HEADS, GQA_GROUP, GQA_HEAD_DIM), k, v

    q_lat, k_lat, v_lat = project(h_lat, True)
    q_ctx, k_ctx, v_ctx = project(h_ctx, False)
    k_all = jnp.concatenate([k_ctx, k_lat], axis=1)
    v_all = jnp.concatenate([v_ctx, v_lat], axis=1)
    y_lat = block_attention(q_lat, k_all, v_all) @ w_o
    y_ctx = block_attention(q_ctx, k_ctx, v_ctx) @ w_o if need_ctx else None
    return y_lat, y_ctx

def mla_mixer(h_lat, h_ctx, w_in, q_norm, kv_norm, w_uq, w_ukv, w_o, rope, need_ctx):
    def project(h, rotate):
        b, n, _ = h.shape
        cq, ckv, k_pe = jnp.split(h @ w_in, [MLA_Q_RANK, MLA_Q_RANK + MLA_KV_RANK], axis=-1)
        q = (rms_norm(cq, q_norm) @ w_uq).reshape(b, n, MLA_HEADS, MLA_NOPE_DIM + MLA_ROPE_DIM)
        q_nope, q_pe = jnp.split(q, [MLA_NOPE_DIM], axis=-1)
        kv = (rms_norm(ckv, kv_norm) @ w_ukv).reshape(b, n, MLA_HEADS, MLA_NOPE_DIM + MLA_V_DIM)
        k_nope, v = jnp.split(kv, [MLA_NOPE_DIM], axis=-1)
        k_pe = k_pe[:, :, None, :]
        if rotate:
            q_pe = apply_grid_rope(q_pe, rope)
            k_pe = apply_grid_rope(k_pe, rope)
        q = jnp.concatenate([q_nope, q_pe], axis=-1)[:, :, :, None, :]
        k = jnp.concatenate([k_nope, jnp.broadcast_to(k_pe, (b, n, MLA_HEADS, MLA_ROPE_DIM))], axis=-1)
        return q, k, v

    q_lat, k_lat, v_lat = project(h_lat, True)
    q_ctx, k_ctx, v_ctx = project(h_ctx, False)
    k_all = jnp.concatenate([k_ctx, k_lat], axis=1)
    v_all = jnp.concatenate([v_ctx, v_lat], axis=1)
    y_lat = block_attention(q_lat, k_all, v_all) @ w_o
    y_ctx = block_attention(q_ctx, k_ctx, v_ctx) @ w_o if need_ctx else None
    return y_lat, y_ctx

def sq_relu_mlp(h, w1, w2):
    return jnp.square(jax.nn.relu(h @ w1)) @ w2

def first_inputs(seed: int = 0) -> dict:
    key = jax.random.key(seed)
    ks = jax.random.split(key, 20)
    d = D_MODEL
    n_a = (DEPTH + N_MIXERS - 1) // N_MIXERS
    n_b = DEPTH // N_MIXERS

    def w(k, shape, fan_in, gain=1.0):
        return jax.random.normal(k, shape, jnp.float32) * (gain * fan_in ** -0.5)

    def gain_vec(k, shape):
        return 1.0 + 0.02 * jax.random.normal(k, shape, jnp.float32)

    qkv_cols = (GQA_HEADS + 2 * GQA_KV_HEADS) * GQA_HEAD_DIM
    mla_in_cols = MLA_Q_RANK + MLA_KV_RANK + MLA_ROPE_DIM
    return {
        "x": jax.random.normal(ks[0], (BATCH, SEQ, d), jnp.float32),
        "c": jax.random.normal(ks[1], (BATCH, d), jnp.float32),
        "ctx": jax.random.normal(ks[2], (BATCH, CTX_LEN, d), jnp.float32),
        "c_ctx": jax.random.normal(ks[3], (d,), jnp.float32),
        "w_ada": w(ks[4], (DEPTH, d, 6 * d), d),
        "b_ada": 0.02 * jax.random.normal(ks[5], (DEPTH, 6 * d), jnp.float32),
        "ln_g": gain_vec(ks[6], (DEPTH, 2, d)),
        "ln_b": 0.02 * jax.random.normal(ks[7], (DEPTH, 2, d), jnp.float32),
        "mlp_w1": w(ks[8], (DEPTH, d, FFN_HIDDEN), d),
        "mlp_w2": w(ks[9], (DEPTH, FFN_HIDDEN, d), FFN_HIDDEN, DEEPNORM_BETA),
        "gqa_w_qkv": w(ks[10], (n_a, d, qkv_cols), d),
        "gqa_q_norm": gain_vec(ks[11], (n_a, GQA_HEAD_DIM)),
        "gqa_k_norm": gain_vec(ks[12], (n_a, GQA_HEAD_DIM)),
        "gqa_w_o": w(ks[13], (n_a, GQA_HEADS * GQA_HEAD_DIM, d), GQA_HEADS * GQA_HEAD_DIM, DEEPNORM_BETA),
        "mla_w_in": w(ks[14], (n_b, d, mla_in_cols), d),
        "mla_q_norm": gain_vec(ks[15], (n_b, MLA_Q_RANK)),
        "mla_kv_norm": gain_vec(ks[16], (n_b, MLA_KV_RANK)),
        "mla_w_uq": w(ks[17], (n_b, MLA_Q_RANK, MLA_HEADS * (MLA_NOPE_DIM + MLA_ROPE_DIM)), MLA_Q_RANK),
        "mla_w_ukv": w(ks[18], (n_b, MLA_KV_RANK, MLA_HEADS * (MLA_NOPE_DIM + MLA_V_DIM)), MLA_KV_RANK),
        "mla_w_o": w(ks[19], (n_b, MLA_HEADS * MLA_V_DIM, d), MLA_HEADS * MLA_V_DIM, DEEPNORM_BETA),
    }

def first_block(x, c, ctx, c_ctx, w_ada, b_ada, ln_g, ln_b, mlp_w1, mlp_w2,
              gqa_w_qkv, gqa_q_norm, gqa_k_norm, gqa_w_o,
              mla_w_in, mla_q_norm, mla_kv_norm, mla_w_uq, mla_w_ukv, mla_w_o):
    n_tok = x.shape[1]
    rope_gqa = grid_rope_tables(n_tok, GQA_HEAD_DIM)
    rope_mla = grid_rope_tables(n_tok, MLA_ROPE_DIM)
    alpha = DEEPNORM_ALPHA
    silu_c = jax.nn.silu(c)
    silu_cc = jax.nn.silu(c_ctx)
    xc = ctx
    for i in range(DEPTH):
        need_ctx = i < DEPTH - 1
        mod_lat = (silu_c @ w_ada[i] + b_ada[i])[:, None, :]
        mod_ctx = silu_cc @ w_ada[i] + b_ada[i]
        sh_a, sc_a, g_a, sh_m, sc_m, g_m = jnp.split(mod_lat, 6, axis=-1)
        csh_a, csc_a, cg_a, csh_m, csc_m, cg_m = jnp.split(mod_ctx, 6, axis=-1)

        h_lat = x * (1.0 + sc_a) + sh_a
        h_ctx = xc * (1.0 + csc_a) + csh_a
        j = i // N_MIXERS
        if i % N_MIXERS == 0:
            y_lat, y_ctx = gqa_mixer(h_lat, h_ctx, gqa_w_qkv[j], gqa_q_norm[j], gqa_k_norm[j],
                                     gqa_w_o[j], rope_gqa, need_ctx)
        else:
            y_lat, y_ctx = mla_mixer(h_lat, h_ctx, mla_w_in[j], mla_q_norm[j], mla_kv_norm[j],
                                     mla_w_uq[j], mla_w_ukv[j], mla_w_o[j], rope_mla, need_ctx)

        x = layer_norm(alpha * x + g_a * y_lat, ln_g[i, 0], ln_b[i, 0])
        x = layer_norm(alpha * x + g_m * sq_relu_mlp(x * (1.0 + sc_m) + sh_m, mlp_w1[i], mlp_w2[i]),
                       ln_g[i, 1], ln_b[i, 1])
        if need_ctx:
            xc = layer_norm(alpha * xc + cg_a * y_ctx, ln_g[i, 0], ln_b[i, 0])
            xc = layer_norm(alpha * xc + cg_m * sq_relu_mlp(xc * (1.0 + csc_m) + csh_m, mlp_w1[i], mlp_w2[i]),
                            ln_g[i, 1], ln_b[i, 1])
    return x


DEPTH_2 = 1

GLA_HEADS = 4
GLA_DK = D_MODEL // 16
GLA_DV = D_MODEL // 8
GLA_RANK = 16
GLA_GATE_NORM = 16.0
ML_HEADS = 4
ML_DK = D_MODEL // 16
ML_DV = D_MODEL // 8
ML_CONV = 4
S5_GROUP = 16
S5_WIDTH = D_MODEL // 2
S5_GROUPS = S5_WIDTH // S5_GROUP
S5_STATE = 64
S5_DT_MIN = 0.001
S5_DT_MAX = 0.1
CHUNK = 64
FFN_HIDDEN_2 = ((8 * D_MODEL + 767) // 768) * 256
N_BRANCH = 3
RMS_EPS = 1e-6

IN_SIZES = (
    GLA_HEADS * GLA_DK,
    GLA_HEADS * GLA_DK,
    GLA_HEADS * GLA_DV,
    GLA_RANK,
    GLA_HEADS * GLA_DV,
    ML_HEADS * ML_DK,
    ML_HEADS * ML_DK,
    ML_HEADS * ML_DV,
    ML_HEADS,
    ML_HEADS,
    ML_HEADS * ML_DV,
    S5_WIDTH,
    N_BRANCH * D_MODEL,
)
IN_DIM = sum(IN_SIZES)


def rms_norm_2(x, w):
    xf = x.astype(jnp.float32)
    y = xf * lax.rsqrt(jnp.mean(xf * xf, axis=-1, keepdims=True) + RMS_EPS)
    return (y * w.astype(jnp.float32)).astype(x.dtype)

def _split(z, sizes):
    out, start = [], 0
    for s in sizes:
        out.append(z[..., start:start + s])
        start += s
    return out

def _heads(a, n):
    return a.reshape(a.shape[0], a.shape[1], n, -1)

def _to_chunks(a):
    b, t, h, d = a.shape
    return a.reshape(b, t // CHUNK, CHUNK, h, d).transpose(1, 0, 3, 2, 4)

def _from_chunks(a):
    n, b, h, l, d = a.shape
    return a.transpose(1, 0, 3, 2, 4).reshape(b, n * l, h, d)

def gla_attention(q, k, v, g):
    out_dtype = v.dtype
    f32 = jnp.float32
    bsz, _, heads, dk = q.shape
    dv = v.shape[-1]
    qc, kc, vc, gc = (_to_chunks(a.astype(f32)) for a in (q * dk ** -0.5, k, v, g))
    causal = jnp.tril(jnp.ones((CHUNK, CHUNK), dtype=bool))

    def step(state, inp):
        qi, ki, vi, gi = inp
        cum = jnp.cumsum(gi, axis=2)
        o_inter = jnp.einsum('bhld,bhdv->bhlv', qi * jnp.exp(cum), state)
        rel = cum[:, :, :, None, :] - cum[:, :, None, :, :]
        decay = jnp.exp(jnp.where(causal[:, :, None], rel, -jnp.inf))
        scores = jnp.einsum('bhid,bhjd,bhijd->bhij', qi, ki, decay)
        o = o_inter + jnp.einsum('bhij,bhjv->bhiv', scores, vi)
        last = cum[:, :, -1:, :]
        state = (jnp.exp(last[:, :, 0, :])[..., None] * state
                 + jnp.einsum('bhjd,bhjv->bhdv', ki * jnp.exp(last - cum), vi))
        return state, o

    s0 = jnp.zeros((bsz, heads, dk, dv), f32)
    _, o = lax.scan(step, s0, (qc, kc, vc, gc))
    return _from_chunks(o).astype(out_dtype)

def mlstm_memory(q, k, v, i_pre, f_pre):
    out_dtype = v.dtype
    f32 = jnp.float32
    bsz, _, heads, dk = q.shape
    dv = v.shape[-1]
    log_f = jax.nn.log_sigmoid(f_pre.astype(f32))
    qc, kc, vc = (_to_chunks(a.astype(f32)) for a in (q, k * dk ** -0.5, v))
    ic, fc = (_to_chunks(a.astype(f32)[..., None])[..., 0] for a in (i_pre, log_f))
    causal = jnp.tril(jnp.ones((CHUNK, CHUNK), dtype=bool))

    def step(carry, inp):
        mem, norm, m_prev = carry
        qi, ki, vi, ii, lfi = inp
        b = jnp.cumsum(lfi, axis=-1)
        a_inter = b + m_prev[..., None]
        d_intra = jnp.where(causal, b[..., :, None] - b[..., None, :] + ii[..., None, :], -jnp.inf)
        m_t = jnp.maximum(a_inter, jnp.max(d_intra, axis=-1))
        w_inter = jnp.exp(a_inter - m_t)
        scores = jnp.einsum('bhtd,bhsd->bhts', qi, ki) * jnp.exp(d_intra - m_t[..., None])
        num = (w_inter[..., None] * jnp.einsum('bhtd,bhdv->bhtv', qi, mem)
               + jnp.einsum('bhts,bhsv->bhtv', scores, vi))
        den = w_inter * jnp.einsum('bhtd,bhd->bht', qi, norm) + jnp.sum(scores, axis=-1)
        h = num / jnp.maximum(jnp.abs(den), jnp.exp(-m_t))[..., None]
        m_new = m_t[..., -1]
        carry_decay = jnp.exp(b[..., -1] + m_prev - m_new)
        w_key = jnp.exp(b[..., -1:] - b + ii - m_new[..., None])
        mem = carry_decay[..., None, None] * mem + jnp.einsum('bhs,bhsd,bhsv->bhdv', w_key, ki, vi)
        norm = carry_decay[..., None] * norm + jnp.einsum('bhs,bhsd->bhd', w_key, ki)
        return (mem, norm, m_new), h

    carry0 = (jnp.zeros((bsz, heads, dk, dv), f32),
              jnp.zeros((bsz, heads, dk), f32),
              jnp.zeros((bsz, heads), f32))
    _, h = lax.scan(step, carry0, (qc, kc, vc, ic, fc))
    return _from_chunks(h).astype(out_dtype)

def _complex_linear_combine(earlier, later):
    a1r, a1i, b1r, b1i = earlier
    a2r, a2i, b2r, b2i = later
    return (a2r * a1r - a2i * a1i,
            a2r * a1i + a2i * a1r,
            a2r * b1r - a2i * b1i + b2r,
            a2r * b1i + a2i * b1r + b2i)

def s5_ssm(u, lam_re, lam_im, log_step, b_re, b_im, c_re, c_im, d_skip):
    out_dtype = u.dtype
    f32 = jnp.float32
    bsz, t, _ = u.shape
    uf = u.astype(f32).reshape(bsz, t, S5_GROUPS, S5_GROUP)
    lam_re = jnp.minimum(lam_re.astype(f32), -1e-4)
    lam_im = lam_im.astype(f32)
    dt = jnp.exp(log_step.astype(f32))[:, None]
    mag = jnp.exp(lam_re * dt)
    abar_re = mag * jnp.cos(lam_im * dt)
    abar_im = mag * jnp.sin(lam_im * dt)
    inv = 1.0 / (lam_re * lam_re + lam_im * lam_im)
    z_re = ((abar_re - 1.0) * lam_re + abar_im * lam_im) * inv
    z_im = (abar_im * lam_re - (abar_re - 1.0) * lam_im) * inv
    b_re = b_re.astype(f32)
    b_im = b_im.astype(f32)
    bbar_re = z_re[..., None] * b_re - z_im[..., None] * b_im
    bbar_im = z_re[..., None] * b_im + z_im[..., None] * b_re
    bu_re = jnp.einsum('gpc,btgc->btgp', bbar_re, uf)
    bu_im = jnp.einsum('gpc,btgc->btgp', bbar_im, uf)
    a_re = jnp.broadcast_to(abar_re, (1, t) + abar_re.shape)
    a_im = jnp.broadcast_to(abar_im, (1, t) + abar_im.shape)
    _, _, x_re, x_im = lax.associative_scan(_complex_linear_combine, (a_re, a_im, bu_re, bu_im), axis=1)
    y = (jnp.einsum('gcp,btgp->btgc', c_re.astype(f32), x_re)
         - jnp.einsum('gcp,btgp->btgc', c_im.astype(f32), x_im))
    y = y.reshape(bsz, t, S5_WIDTH) + d_skip.astype(f32) * u.astype(f32)
    return y.astype(out_dtype)

def causal_dwconv(u, w, b):
    k = w.shape[0]
    y = lax.conv_general_dilated(u, w[:, None, :], window_strides=(1,), padding=[(k - 1, 0)],
                                 dimension_numbers=('NWC', 'WIO', 'NWC'),
                                 feature_group_count=u.shape[-1])
    return y + b

def hybrid_mixer(h, w_in, gla_a2, gla_a_b, gla_norm_w, ml_conv_w, ml_conv_b, ml_i_b, ml_f_b,
                 s5_lam_re, s5_lam_im, s5_log_step, s5_b_re, s5_b_im, s5_c_re, s5_c_im, s5_d,
                 s5_glu_w, s5_glu_b, proj_gla, proj_ml, proj_s5, branch_gate_b, w_out):
    bsz, t, _ = h.shape
    z = h @ w_in
    gq, gk, gv, ga, gr, mq, mk, mv, mi, mf, mo, su, zg = _split(z, IN_SIZES)

    g_log = jax.nn.log_sigmoid((ga @ gla_a2 + gla_a_b).astype(jnp.float32)) / GLA_GATE_NORM
    o_gla = gla_attention(_heads(gq, GLA_HEADS), _heads(gk, GLA_HEADS), _heads(gv, GLA_HEADS),
                          _heads(g_log, GLA_HEADS))
    o_gla = rms_norm_2(o_gla, gla_norm_w.reshape(GLA_HEADS, GLA_DV)).reshape(bsz, t, -1)
    y_gla = o_gla * jax.nn.silu(gr)

    qk = jax.nn.silu(causal_dwconv(jnp.concatenate([mq, mk], axis=-1), ml_conv_w, ml_conv_b))
    mq = qk[..., :ML_HEADS * ML_DK]
    mk = qk[..., ML_HEADS * ML_DK:]
    h_ml = mlstm_memory(_heads(mq, ML_HEADS), _heads(mk, ML_HEADS), _heads(mv, ML_HEADS),
                        mi + ml_i_b, mf + ml_f_b)
    y_ml = jax.nn.sigmoid(mo) * h_ml.reshape(bsz, t, -1)

    y_s5 = jax.nn.gelu(s5_ssm(su, s5_lam_re, s5_lam_im, s5_log_step, s5_b_re, s5_b_im,
                              s5_c_re, s5_c_im, s5_d))
    y_s5 = y_s5 * jax.nn.sigmoid(y_s5 @ s5_glu_w + s5_glu_b)

    gates = jax.nn.sigmoid(zg + branch_gate_b).reshape(bsz, t, N_BRANCH, D_MODEL)
    merged = (gates[:, :, 0] * (y_gla @ proj_gla)
              + gates[:, :, 1] * (y_ml @ proj_ml)
              + gates[:, :, 2] * (y_s5 @ proj_s5))
    return merged @ w_out

def swiglu_ffn(h, w_in, w_out):
    gate, up = jnp.split(h @ w_in, 2, axis=-1)
    return (jax.nn.silu(gate) * up) @ w_out

def second_inputs(seed: int = 0) -> dict:
    key = jax.random.key(seed)
    keys = list(jax.random.split(key, 48))

    def normal(shape, scale):
        return scale * jax.random.normal(keys.pop(), shape, jnp.float32)

    def uniform(shape):
        return jax.random.uniform(keys.pop(), shape, jnp.float32)

    def gain(shape):
        return 1.0 + normal(shape, 0.05)

    L, D = DEPTH_2, D_MODEL
    glw = GLA_HEADS * GLA_DV
    mlw = ML_HEADS * ML_DV
    n_idx = jnp.arange(S5_STATE, dtype=jnp.float32)
    log_lo, log_hi = math.log(S5_DT_MIN), math.log(S5_DT_MAX)
    return {
        'x': normal((BATCH, SEQ, D), 1.0),
        'c': normal((BATCH, D), 1.0),
        'ada_w': normal((L, D, 6 * D), 0.1 * D ** -0.5),
        'ada_b': normal((L, 6 * D), 0.01),
        'pre1_w': gain((L, D)),
        'post1_w': gain((L, D)),
        'pre2_w': gain((L, D)),
        'post2_w': gain((L, D)),
        'w_in': normal((L, D, IN_DIM), D ** -0.5),
        'gla_a2': normal((L, GLA_RANK, GLA_HEADS * GLA_DK), GLA_RANK ** -0.5),
        'gla_a_b': normal((L, GLA_HEADS * GLA_DK), 0.1),
        'gla_norm_w': gain((L, glw)),
        'ml_conv_w': normal((L, ML_CONV, 2 * ML_HEADS * ML_DK), ML_CONV ** -0.5),
        'ml_conv_b': normal((L, 2 * ML_HEADS * ML_DK), 0.01),
        'ml_i_b': normal((L, ML_HEADS), 0.1),
        'ml_f_b': 3.0 + 3.0 * uniform((L, ML_HEADS)),
        's5_lam_re': -0.5 + normal((L, S5_GROUPS, S5_STATE), 0.01),
        's5_lam_im': math.pi * n_idx + normal((L, S5_GROUPS, S5_STATE), 0.01),
        's5_log_step': log_lo + (log_hi - log_lo) * uniform((L, S5_GROUPS)),
        's5_b_re': normal((L, S5_GROUPS, S5_STATE, S5_GROUP), (2 * S5_GROUP) ** -0.5),
        's5_b_im': normal((L, S5_GROUPS, S5_STATE, S5_GROUP), (2 * S5_GROUP) ** -0.5),
        's5_c_re': normal((L, S5_GROUPS, S5_GROUP, S5_STATE), S5_STATE ** -0.5),
        's5_c_im': normal((L, S5_GROUPS, S5_GROUP, S5_STATE), S5_STATE ** -0.5),
        's5_d': normal((L, S5_WIDTH), 1.0),
        's5_glu_w': normal((L, S5_WIDTH, S5_WIDTH), S5_WIDTH ** -0.5),
        's5_glu_b': normal((L, S5_WIDTH), 0.01),
        'proj_gla': normal((L, glw, D), glw ** -0.5),
        'proj_ml': normal((L, mlw, D), mlw ** -0.5),
        'proj_s5': normal((L, S5_WIDTH, D), S5_WIDTH ** -0.5),
        'branch_gate_b': normal((L, N_BRANCH * D), 0.01),
        'w_out': normal((L, D, D), D ** -0.5),
        'ffn_w_in': normal((L, D, 2 * FFN_HIDDEN_2), D ** -0.5),
        'ffn_w_out': normal((L, FFN_HIDDEN_2, D), FFN_HIDDEN_2 ** -0.5),
    }

def second_block(x, c, ada_w, ada_b, pre1_w, post1_w, pre2_w, post2_w, w_in, gla_a2, gla_a_b,
              gla_norm_w, ml_conv_w, ml_conv_b, ml_i_b, ml_f_b, s5_lam_re, s5_lam_im, s5_log_step,
              s5_b_re, s5_b_im, s5_c_re, s5_c_im, s5_d, s5_glu_w, s5_glu_b, proj_gla, proj_ml,
              proj_s5, branch_gate_b, w_out, ffn_w_in, ffn_w_out):
    c_act = jax.nn.silu(c)
    for l in range(DEPTH_2):
        mod = c_act @ ada_w[l] + ada_b[l]
        sh1, sc1, gt1, sh2, sc2, gt2 = [m[:, None, :] for m in jnp.split(mod, 6, axis=-1)]

        h = rms_norm_2(x, pre1_w[l]) * (1.0 + sc1) + sh1
        y = hybrid_mixer(h, w_in[l], gla_a2[l], gla_a_b[l], gla_norm_w[l], ml_conv_w[l], ml_conv_b[l],
                         ml_i_b[l], ml_f_b[l], s5_lam_re[l], s5_lam_im[l], s5_log_step[l],
                         s5_b_re[l], s5_b_im[l], s5_c_re[l], s5_c_im[l], s5_d[l], s5_glu_w[l],
                         s5_glu_b[l], proj_gla[l], proj_ml[l], proj_s5[l], branch_gate_b[l], w_out[l])
        x = x + (1.0 + gt1) * rms_norm_2(y, post1_w[l])

        h = rms_norm_2(x, pre2_w[l]) * (1.0 + sc2) + sh2
        y = swiglu_ffn(h, ffn_w_in[l], ffn_w_out[l])
        x = x + (1.0 + gt2) * rms_norm_2(y, post2_w[l])
    return x


def setup_inputs(seed=0):
    out = dict(first_inputs(seed))
    for name, value in second_inputs(seed + 1).items():
        if name != "x":
            out[name + "_2"] = value
    return out


def reference(
    x, c, ctx, c_ctx, w_ada, b_ada, ln_g, ln_b, mlp_w1, mlp_w2, gqa_w_qkv, gqa_q_norm,
    gqa_k_norm, gqa_w_o, mla_w_in, mla_q_norm, mla_kv_norm, mla_w_uq, mla_w_ukv, mla_w_o, c_2,
    ada_w_2, ada_b_2, pre1_w_2, post1_w_2, pre2_w_2, post2_w_2, w_in_2, gla_a2_2, gla_a_b_2,
    gla_norm_w_2, ml_conv_w_2, ml_conv_b_2, ml_i_b_2, ml_f_b_2, s5_lam_re_2, s5_lam_im_2,
    s5_log_step_2, s5_b_re_2, s5_b_im_2, s5_c_re_2, s5_c_im_2, s5_d_2, s5_glu_w_2, s5_glu_b_2,
    proj_gla_2, proj_ml_2, proj_s5_2, branch_gate_b_2, w_out_2, ffn_w_in_2, ffn_w_out_2,
):
    x = first_block(
        x, c, ctx, c_ctx, w_ada, b_ada, ln_g, ln_b, mlp_w1, mlp_w2, gqa_w_qkv, gqa_q_norm,
        gqa_k_norm, gqa_w_o, mla_w_in, mla_q_norm, mla_kv_norm, mla_w_uq, mla_w_ukv, mla_w_o,
    )
    return second_block(
        x, c_2, ada_w_2, ada_b_2, pre1_w_2, post1_w_2, pre2_w_2, post2_w_2, w_in_2, gla_a2_2,
        gla_a_b_2, gla_norm_w_2, ml_conv_w_2, ml_conv_b_2, ml_i_b_2, ml_f_b_2, s5_lam_re_2,
        s5_lam_im_2, s5_log_step_2, s5_b_re_2, s5_b_im_2, s5_c_re_2, s5_c_im_2, s5_d_2,
        s5_glu_w_2, s5_glu_b_2, proj_gla_2, proj_ml_2, proj_s5_2, branch_gate_b_2, w_out_2,
        ffn_w_in_2, ffn_w_out_2,
    )


_drawn_inputs = setup_inputs


def setup_inputs(seed=0):
    import zlib

    import numpy as np

    out = dict(_drawn_inputs(seed))
    spreads = {}
    factors = {'gqa_q_norm': 8.0,
     'gqa_k_norm': 8.0,
     'mla_q_norm': 8.0,
     'mla_kv_norm': 8.0,
     'ml_conv_b_2': 2.891,
     'ml_i_b_2': 5.979,
     's5_lam_re_2': 200.0,
     's5_glu_b_2': 38.403,
     'branch_gate_b_2': 8.0,
     's5_lam_im_2': 34.496,
     's5_log_step_2': 44.32,
     's5_b_re_2': 48.704,
     's5_b_im_2': 45.248,
     's5_c_re_2': 45.128,
     's5_c_im_2': 47.688}
    for name, (base, spread) in spreads.items():
        noise = np.random.default_rng([zlib.crc32(name.encode()), seed]).standard_normal(out[name].shape)
        drawn = base * np.exp(spread * noise) if base else spread * noise
        out[name] = jnp.asarray(drawn.astype(out[name].dtype))
    for name, factor in factors.items():
        out[name] = (out[name] * factor).astype(out[name].dtype)
    return out
```

```python
from contextlib import ExitStack

import numpy as np

import concourse.bass as bass
from concourse import mybir

F32 = mybir.dt.float32
I8 = mybir.dt.uint8
I32 = mybir.dt.int32
ALU = mybir.AluOpType
ACT = mybir.ActivationFunctionType
AX = mybir.AxisListType
D = 1024
LAT, CTX = 512, 256
TOK = LAT + CTX
SEG = [(0, LAT), (LAT, CTX)]
ALPHA = (2.0 * 2) ** 0.25
EPS = 1e-6
PI = float(np.pi)


class Token:

    def __init__(self, eng, n):
        self.eng, self.n, self.value = eng, n, None


class DmaToken:
    def __init__(self, sem, value):
        self.sem, self.value = sem, value


class Queue:

    def __init__(self, name):
        self.name, self.ops, self.sem = name, [], None

    def __call__(self, fn, *waits):
        t = Token(self, len(self.ops))
        self.ops.append((flat(waits), fn, t, None))
        return t

    def last(self):
        return [self.ops[-1][2]] if self.ops else []


def flat(x):
    if x is None:
        return []
    if isinstance(x, (list, tuple)):
        return [z for y in x for z in flat(y)]
    return [x]


class Program:
    def __init__(self, nc, ctx):
        self.nc, self.ctx = nc, ctx
        self.pe, self.act, self.dve, self.pool, self.sp = (Queue(n) for n in ("pe", "act", "dve", "pool", "sp"))
        self.queues = [self.pe, self.act, self.dve, self.pool, self.sp]
        self.counts = {}
        self.nsem = 0

    def sem(self, name):
        self.nsem += 1
        return self.ctx.enter_context(self.nc.semaphore(name))

    def dma(self, queue, sem, out, in_, *waits):
        v = self.counts.get(id(sem), 0) + 16
        self.counts[id(sem)] = v
        queue.ops.append((flat(waits), lambda e: e.dma_start(out, in_), None, sem))
        return DmaToken(sem, v)

    def fence(self):
        return [t for q in (self.pe, self.act, self.dve, self.pool) for t in q.last()
                if isinstance(t, Token)]

    def emit(self, block, ends):
        used = {id(t) for q in self.queues for w, _, _, _ in q.ops for t in w}
        for q in self.queues:
            q.sem = self.sem("done_" + q.name)
            n = 0
            for _, _, t, _ in q.ops:
                if t is not None:
                    if id(t) in used:
                        n += 1
                        t.value = n

        def body(q):
            def run(eng):
                seen = {}
                for waits, fn, t, dsem in q.ops:
                    need = {}
                    for w in waits:
                        s = w.eng.sem if isinstance(w, Token) else w.sem
                        if w.value > max(seen.get(id(s), 0), need.get(id(s), (None, 0))[1]):
                            need[id(s)] = (s, w.value)
                    for k, (s, v) in need.items():
                        eng.wait_ge(s, v)
                        seen[k] = v
                    ins = fn(eng)
                    if dsem is not None:
                        ins.then_inc(dsem, 16)
                    elif t.value is not None:
                        ins.then_inc(q.sem, 1)
                if q is self.sp:
                    for t in ends:
                        eng.wait_ge(t.sem, t.value)
            return run

        block.tensor(body(self.pe))
        block.scalar(body(self.act))
        block.vector(body(self.dve))
        block.gpsimd(body(self.pool))
        block.sync(body(self.sp))


class Ring:

    def __init__(self, items, free=()):
        self.free = [(i, list(free)) for i in items]

    def take(self):
        return self.free.pop(0)

    def give(self, item, *tokens):
        self.free.append((item, flat(tokens)))


class Banks:

    def __init__(self, n=8):
        self.free = [(i, []) for i in range(n)]

    def take(self):
        return self.free.pop(0)

    def pair(self):
        for i, (b, w) in enumerate(self.free):
            for j, (c, v) in enumerate(self.free):
                if b % 2 == 0 and c == b + 1:
                    for x in sorted((i, j), reverse=True):
                        self.free.pop(x)
                    return b, w + v
        raise RuntimeError("no pair of banks")

    def give(self, b, *tokens):
        self.free.append((b, flat(tokens)))

    def give_pair(self, b, *tokens):
        self.give(b, *tokens)
        self.give(b + 1, *tokens)


def rope_tables(rot, copies, pad):
    n = np.arange(LAT)
    row, col = (n // 64).astype(np.float32), (n % 64).astype(np.float32)
    axis = rot // 2
    inv = (np.float32(10000.0) ** (-np.arange(0, axis, 2, dtype=np.float32) / np.float32(axis))).astype(np.float32)
    parts = []
    for pos in (row, col):
        ang = (pos[:, None] * inv[None, :]).astype(np.float32).T
        parts += [ang, ang]
    ang = np.concatenate(parts, 0)
    c, s = np.cos(ang).astype(np.float32), np.sin(ang).astype(np.float32)
    if pad:
        c = np.concatenate([np.ones((pad, LAT), np.float32), c], 0)
        s = np.concatenate([np.zeros((pad, LAT), np.float32), s], 0)
    return np.tile(c, (copies, 1)), np.tile(s, (copies, 1))


def rope_swap(rot, copies, pad):
    q = rot // 4
    n = (rot + pad) * copies
    m = np.zeros((n, n), np.float32)
    for c in range(copies):
        for half in range(2):
            o = c * (rot + pad) + pad + half * 2 * q
            for i in range(q):
                m[o + q + i, o + i] = -1.0
                m[o + i, o + q + i] = 1.0
    return m


def constants():
    p = np.arange(128)
    k = {}
    k["ident"] = np.eye(128, dtype=np.float32)
    k["ones"] = np.ones((128, 128), np.float32)
    k["mean"] = np.full((128, 128), 1.0 / 1024, np.float32)
    k["head64"] = (p[:, None] // 64 == p[None, :] // 64).astype(np.float32)
    k["swap64"] = rope_swap(64, 2, 0)
    s96 = np.zeros((128, 128), np.float32)
    s96[:96, :96] = rope_swap(32, 1, 64)
    k["swap96"] = s96
    k["causal"] = (p[:, None] <= p[None, :]).astype(np.float32)
    k["cmask"] = ((p[:, None] // 64) == (p[None, :] // 16) % 2).astype(np.float32)
    sel = np.zeros((128, 512), np.float32)
    for h in range(4):
        sel[h, h * 128:(h + 1) * 128] = 1.0
    mats = np.concatenate([k[n] for n in MATS] + [sel], 1)
    c64, s64 = rope_tables(64, 2, 0)
    c96, s96t = rope_tables(32, 1, 64)
    z = np.zeros((32, LAT), np.float32)
    turn = np.stack([c64, s64, np.concatenate([c96, z]), np.concatenate([s96t, z])])
    masks = []
    for h in (64, 32, 16, 8, 4, 2, 1):
        b = p // (2 * h)
        masks.append((b[:, None] == b[None, :]) & ((p % (2 * h)) < h)[:, None] & ((p % (2 * h)) >= h)[None, :])
    masks.append(np.eye(128, dtype=bool))
    masks = np.concatenate(masks, 1).astype(np.float32)
    return {"k_mats": mats, "k_turn": turn, "k_masks": masks}


MATS = ["ident", "ones", "mean", "head64", "swap64", "swap96", "causal", "cmask"]


def build(nc, a, out, parts=("l0", "l1", "mix", "ffn"), dbg=None):
    ctx = ExitStack()
    with ctx:
        P = Program(nc, ctx)
        pe, act, dve, pool, sp = P.queues

        def cp(q, out_, in_, *w):
            return q(lambda e: e.tensor_copy(out_, in_), *w)

        def fill(q, out_, v, *w):
            return q(lambda e: e.memset(out_, v), *w)

        def recip(q, out_, in_, *w):
            return q(lambda e: e.reciprocal(out_, in_), *w)

        def scan(q, out_, d0, d1, first, o0, o1, *w):
            return q(lambda e: e.tensor_tensor_scan(out_, d0, d1, first, o0, o1), *w)

        def cpred(q, out_, mask, data, *w):
            return q(lambda e: e.copy_predicated(out_, mask, data), *w)

        def trp(q, out_, in_, idn, *w):
            return q(lambda e: e.transpose(out_, in_, idn), *w)

        def sb(name, shape, dt=F32):
            return ctx.enter_context(nc.sbuf_tensor(name, shape, dt))

        X = sb("X", [128, 8, TOK])
        H = sb("H", [128, 8, TOK])
        AR = sb("AR", [128, 24576])
        WR = sb("WR", [128, 5, 2048])
        EB = sb("EB", [128, 2048])
        KM = sb("KM", [128, 8 * 128])
        MOD = sb("MOD", [128, 2, 48, 2])
        SM = sb("SM", [128, 640])
        STATS = sb("STAT", [128, 1280])
        STAT = [STATS[:, 0:512], STATS[:, 512:1024], STATS[:, 1024:1280]]
        PS = ctx.enter_context(nc.psum_tensor("PS", [128, 8, 512], F32))
        EDR = nc.dram_tensor("e_scratch", (16, 128, 1024), F32, kind="Internal").ap()
        mat = {n: KM[:, i * 128:(i + 1) * 128] for i, n in enumerate(MATS)}
        banks = Banks()

        def ps(b, n=512, rows=slice(0, 128)):
            return PS[rows, b, 0:n]

        def ps2(b, rows=slice(0, 128)):
            return PS[rows, b:b + 2, :].rearrange("p a b -> p (a b)")

        smo, smn = {}, [0]

        def col(name, n, rows=slice(0, 128)):
            if name not in smo:
                smo[name] = smn[0]
                smn[0] += n
                assert smn[0] <= 620
            o = smo[name]
            return SM[rows, o:o + n]

        s_const, s_rows = P.sem("s_const"), P.sem("s_rows")
        ROWS = EB[:, 0:384].rearrange("p (g n) -> p g n", n=128)
        tz = fill(dve, EB[:, 0:384], 0.0)
        tC = P.dma(sp, s_const, KM[:, :], a["k_mats"][:, 0:8 * 128])
        trow = []

        def columns(name, n, *srcs):
            if smn[0] // 128 != (smn[0] + n - 1) // 128:
                smn[0] = -(-smn[0] // 128) * 128
            c = col(name, n)
            g, r = divmod(smo[name], 128)
            for src, r0, c0 in srcs:
                trow.append(P.dma(sp, s_rows, ROWS[r + r0:r + r0 + src.shape[0], g, c0:c0 + src.shape[1]], src, tz))
            return c

        def rows_of(v):
            return v.rearrange("(f p) -> f p", p=128)

        def one(v):
            return v.rearrange("(o p) -> o p", o=1)

        cvec = columns("cvec", 24, (rows_of(a["c"][0]), 0, 0), (rows_of(a["c_ctx"]), 8, 0),
                       (rows_of(a["c_2"][0]), 16, 0)).rearrange("p (v f) -> p f v", v=3)
        ADB = [columns(f"adb{i}", 48, (rows_of(a["b_ada"][i]), 0, 0)) for i in range(2)]
        adb2 = columns("adb2", 48, (rows_of(a["ada_b_2"][0]), 0, 0))
        lng = columns("lng", 32, *[(rows_of(a["ln_g"][i, j]), 16 * i + 8 * j, 0) for i in range(2) for j in range(2)])
        lnb = columns("lnb", 32, *[(rows_of(a["ln_b"][i, j]), 16 * i + 8 * j, 0) for i in range(2) for j in range(2)])
        lng, lnb = (v.rearrange("p (i f) -> p i f", f=8) for v in (lng, lnb))
        qg, kg = (columns(n, 1, (one(a[n][0]), 0, 0), (one(a[n][0]), 0, 64)) for n in ("gqa_q_norm", "gqa_k_norm"))
        mqg = columns("mqg", 3, (rows_of(a["mla_q_norm"][0]), 0, 0))
        mkg = columns("mkg", 2, (rows_of(a["mla_kv_norm"][0]), 0, 0))
        nrm = {n: columns(n, 8, (rows_of(a[n][0]), 0, 0)) for n in ("pre1_w_2", "post1_w_2", "pre2_w_2", "post2_w_2")}
        glab = columns("glab", 2, (rows_of(a["gla_a_b_2"][0]), 0, 0))
        glanw = columns("glanw", 4, (rows_of(a["gla_norm_w_2"][0]), 0, 0))
        cw = columns("cw", 16, *[(rows_of(a["ml_conv_w_2"][0, j]), 4 * j, 0) for j in range(4)])
        cw = cw.rearrange("p (j f) -> p j f", f=4)
        cb = columns("cb", 4, (rows_of(a["ml_conv_b_2"][0]), 0, 0))
        ib = columns("ib", 1, (one(a["ml_i_b_2"][0]), 0, 0), (one(a["ml_f_b_2"][0]), 0, 32))
        glub = columns("glub", 4, (rows_of(a["s5_glu_b_2"][0]), 0, 0))
        bgb = columns("bgb", 24, (rows_of(a["branch_gate_b_2"][0]), 0, 0))
        s5d = columns("s5d", 4, (rows_of(a["s5_d_2"][0]), 0, 0))
        lre = columns("lre", 16, (a["s5_lam_re_2"][0].rearrange("(r g) p -> r (g p)", g=2), 0, 0))
        lim = columns("lim", 16, (a["s5_lam_im_2"][0].rearrange("(r g) p -> r (g p)", g=2), 0, 0))
        assert smn[0] <= 384
        smn[0] = 384
        lst = P.dma(sp, s_rows, EB[0:16, 384:386], a["s5_log_step_2"][0].rearrange("(r g) -> r g", g=2))
        lrow = cp(dve, EB[0:16, 512:640].rearrange("p (g n) -> p g n", n=64), EB[0:16, 384:386].unsqueeze(2).to_broadcast([16, 2, 64]), lst)
        dt = col("dt", 16)
        epsc, onec = col("epsc", 1), col("onec", 1)
        t1 = fill(dve, epsc, EPS)
        t2 = fill(dve, onec, 1.0)
        ident = mat["ident"]
        t = trp(pe, PS[:, 0, 0:128], ROWS[:, 0, :], ident, tC, trow, lst, lrow)
        t = trp(pe, PS[:, 0, 128:256], ROWS[:, 1, :], ident)
        t = trp(pe, PS[:, 0, 256:384], ROWS[:, 2, :], ident)
        t = trp(pe, PS[:, 0, 384:400], EB[0:16, 512:640], ident[0:16, 0:16])
        t = cp(dve, SM[:, 0:400], PS[:, 0, 0:400], t)
        b0, _ = banks.take()
        banks.give(b0, t)
        K = [tC, t1, t2, t]

        def mm(out_, l, r, start, stop, *w):
            return pe(lambda e: e.matmul(out_, l, r, start=start, stop=stop), *w)

        def tr(out_, in_, n, *w):
            return trp(pe, out_, in_, mat["ident"][0:n, 0:n], *w)

        def tt(q, out_, i0, i1, op, *w):
            return q(lambda e: e.tensor_tensor(out_, i0, i1, op), *w)

        def ts(q, out_, i0, s1, s2, o0, o1, *w):
            if o1 is None:
                return q(lambda e: e.tensor_scalar(out_, i0, s1, None, o0), *w)
            return q(lambda e: e.tensor_scalar(out_, i0, s1, s2, o0, o1), *w)

        def stt(out_, i0, s, i1, o0, o1, *w):
            return dve(lambda e: e.scalar_tensor_tensor(out=out_, in0=i0, scalar=s, in1=i1, op0=o0, op1=o1), *w)

        def af(out_, in_, f, *w, bias=None, scale=None, accum=None):
            kw = {}
            if bias is not None:
                kw["bias"] = bias
            if scale is not None:
                kw["scale"] = scale
            if accum is not None:
                kw["accum_out"] = accum
            return act(lambda e: e.activation(out_, in_, f, **kw), *w)

        MUL, ADD, SUB, MAX, MIN = ALU.mult, ALU.add, ALU.subtract, ALU.max, ALU.min

        side = []

        def step():
            for g in list(side):
                try:
                    next(g)
                except StopIteration:
                    side.remove(g)

        def drain():
            while side:
                step()

        wsem = [P.sem(f"s_w{i}") for i in range(4)]
        wring = Ring(range(4))

        def weights(src, nk, n):
            slot, w = wring.take()
            v = WR[:, slot, 0:nk * n].rearrange("p (k n) -> p k n", n=n)
            t = P.dma(sp, wsem[slot], v, src.rearrange("(k p) n -> p k n", p=128), w)
            return slot, v, t

        def linear(src, units, nks, rhs, segs, evac):
            for c0, nc_, ms in units:
                accs = {}
                k0 = 0
                kt = sum(nks)
                for nk in nks:
                    slot, v, t = weights(src[k0 * 128:(k0 + nk) * 128, c0:c0 + nc_], nk, nc_)
                    for key, off, M in ms:
                        for s in segs:
                            if k0 == 0:
                                accs[key, s] = banks.take()
                            b, bw = accs[key, s]
                            n = SEG[s][1]
                            for k in range(nk):
                                r, rw = rhs(k0 + k, s)
                                last = mm(ps(b, n, slice(0, M)), v[:, k, off:off + M], r,
                                          k0 + k == 0, k0 + k == kt - 1, t, bw, rw)
                            if k0 + nk == kt:
                                if (key, off, M) == ms[-1] and s == segs[-1]:
                                    wring.give(slot, last)
                                g = evac(key, s, b, last)
                                if g is not None:
                                    side.append(g)
                                step()
                    if k0 + nk < kt:
                        wring.give(slot, last)
                    k0 += nk

        def tiles(c0, n, per=2):
            return [(c0 + i * 128, min(per, n - i) * 128, [(i + j, j * 128, 128) for j in range(min(per, n - i))])
                    for i in range(0, n, per)]

        sil = col("sil", 24).rearrange("p (f v) -> p f v", v=3)
        sx = col("sx", 24).rearrange("p (f v) -> p f v", v=3)
        t = af(sx, cvec, ACT.Exp, K, scale=-1.0)
        t = ts(dve, sx, sx, 1.0, None, ADD, None, t)
        t = recip(dve, sx, sx, t)
        tsil = tt(dve, sil, sx, cvec, MUL, t)
        ROW = sb("ROW", [2, 2, 256])
        rowring = Ring(range(2))
        modt = {}

        def ada(src, nv, v0, bias, dst, adds, c_from, c_to, key):
            for c in range(c_from, c_to):
                slot, v, t = weights(src[:, c * 256:(c + 1) * 256], 8, 256)
                b, bw = banks.take()
                for k in range(8):
                    last = mm(ps(b, 256, slice(0, nv)), sil[:, k, v0:v0 + nv], v[:, k, :], k == 0, k == 7, t, bw, tsil)
                wring.give(slot, last)
                r, rw = rowring.take()
                t = af(ROW[0:nv, r, :], ps(b, 256, slice(0, nv)), ACT.Copy, last, rw)
                banks.give(b, t)
                b, bw = banks.take()
                for j in range(2):
                    last = tr(PS[:, b, j * nv:(j + 1) * nv], ROW[0:nv, r, j * 128:(j + 1) * 128], nv, t, bw, K)
                rowring.give(r, last)
                t = tt(dve, dst[:, 2 * c:2 * c + 2, :], ps(b, 2 * nv).rearrange("p (a v) -> p a v", v=nv),
                       bias[:, 2 * c:2 * c + 2].unsqueeze(2).to_broadcast([128, 2, nv]), ADD, last, K)
                banks.give(b, t)
                for j in adds:
                    if 4 * j <= c < 4 * j + 4:
                        t = ts(dve, dst[:, 2 * c:2 * c + 2, :], dst[:, 2 * c:2 * c + 2, :], 1.0, None, ADD, None, t)
                modt[key] = t

        def ada1(i, c_from, c_to):
            ada(a["w_ada"][i], 2, 0, ADB[i], MOD[:, i, :, :], (1, 4), c_from, c_to, i)

        MOD2 = col("mod2", 48)

        s_x = [P.sem(f"s_x{i}") for i in range(6)]
        xin = AR[:, 0:6 * 1024].rearrange("p (t n) -> p t n", t=6)
        nt = 6 if "l0" in parts or "l1" in parts else 4
        xt = {}
        for t6 in range(nt):
            src = a["x"][0, t6 * 128:(t6 + 1) * 128, :] if t6 < 4 else a["ctx"][0, (t6 - 4) * 128:(t6 - 3) * 128, :]
            td = P.dma(act, s_x[t6], xin[:, t6, :], src)
            for half in range(2):
                b, bw = banks.take()
                for j in range(4):
                    f = half * 4 + j
                    last = tr(PS[:, b, j * 128:(j + 1) * 128], xin[:, t6, f * 128:(f + 1) * 128], 128, td, bw, K)
                dst = X[:, half * 4:half * 4 + 4, t6 * 128:(t6 + 1) * 128]
                src_ = ps(b).rearrange("p (j n) -> p j n", n=128)
                if half:
                    t = cp(dve, dst, src_, last)
                else:
                    t = af(dst, src_, ACT.Copy, last)
                banks.give(b, t)
                for j in range(4):
                    xt.setdefault((half * 4 + j, 0 if t6 < 4 else 1), []).append(t)

        def seg(buf, f, s):
            return buf[:, f, SEG[s][0]:SEG[s][0] + SEG[s][1]]

        ht = {}

        def modulate(i, j, segs, w=()):
            for s in segs:
                for f in range(8):
                    q = dve if f % 2 else pool
                    t = ts(q, seg(H, f, s), seg(X, f, s), MOD[:, i, (3 * j + 1) * 8 + f, s:s + 1],
                           MOD[:, i, 3 * j * 8 + f, s:s + 1], MUL, ADD, xt[f, s], modt[i], w)
                    ht[f, s] = [t]
                    xt[f, s] = [ts(q, seg(X, f, s), seg(X, f, s), ALPHA, None, MUL, None, t)]

        def hrhs(k, s):
            return seg(H, k, s), ht[k, s]

        def add_gated(i, j):
            def evac(f, s, b, t):
                t = stt(seg(X, f, s), ps(b, SEG[s][1]), MOD[:, i, (3 * j + 2) * 8 + f, s:s + 1], seg(X, f, s),
                        MUL, ADD, t, xt[f, s], modt[i])
                banks.give(b, t)
                xt[f, s] = [t]
            return evac

        statt = [[], [], []]

        def rstd(b, n, scale, t, o):
            st = STAT[o][:, 0:n]
            t = af(st, ps(b, n), ACT.Ln, t, statt[o], K, bias=epsc, scale=scale)
            banks.give(b, t)
            return af(st, st, ACT.Exp, t, scale=-0.5)

        def layer_norm(i, segs, tmps):
            for s in segs:
                n = SEG[s][1]
                b, bw = banks.take()
                for f in range(8):
                    last = mm(ps(b, n), mat["mean"], seg(X, f, s), f == 0, f == 7, bw, xt[f, s], K)
                b2, bw2 = banks.take()
                for f in range(8):
                    t = tt(dve, seg(X, f, s), seg(X, f, s), ps(b, n), SUB, last)
                    xt[f, s] = [t]
                    tmp, tw = tmps.take()
                    t2_ = af(tmp[:, 0:n], seg(X, f, s), ACT.Square, t, tw)
                    last2 = mm(ps(b2, n), mat["mean"], tmp[:, 0:n], f == 0, f == 7, bw2, t2_, K)
                    tmps.give(tmp, last2)
                banks.give(b, t)
                tr_ = rstd(b2, n, 1.0, last2, s)
                for f in range(8):
                    t = tt(dve, seg(X, f, s), seg(X, f, s), STAT[s][:, 0:n], MUL, tr_, xt[f, s])
                    xt[f, s] = [ts(pool if f % 2 else dve, seg(X, f, s), seg(X, f, s), lng[:, i, f:f + 1],
                                   lnb[:, i, f:f + 1], MUL, ADD, t, K)]
                statt[s] = [t]

        def token_major(src, c0, n, dst, toks, ntt, w):
            slot, v, t = weights(src[:, c0:c0 + n], 8, n)
            for j in range(ntt):
                b, bw = banks.take()
                s = 0 if j < 4 else 1
                for k in range(8):
                    last = mm(ps(b, n), H[:, k, j * 128:(j + 1) * 128], v[:, k, :], k == 0, k == 7, bw, t, ht[k, s])
                tk = af(dst(j), ps(b, n), ACT.Copy, last, w)
                banks.give(b, tk)
                toks.setdefault(j, []).append(tk)
                step()
            wring.give(slot, last)

        def arena(off, *shape):
            n = int(np.prod(shape))
            v = AR[:, off:off + n]
            if len(shape) == 2:
                v = v.rearrange("p (a b) -> p a b", b=shape[1])
            return v

        def tmp_ring(off, n, fence):
            assert off + n * 512 <= 24576
            return Ring([AR[:, off + i * 512:off + (i + 1) * 512] for i in range(n)], fence)

        def attention(heads, qv, kv, vv, ov, qtiles, keys, Pb, PTb, rw, tag):
            nk = keys[1] // 128
            nq = len(qtiles)
            units = [(h, j) for h in heads for j in range(nq)]
            st = {}
            res = {}

            def first(u):
                h, j = units[u]
                q, qw = qv(h, qtiles[j])
                k, kw = kv(h)
                b, bw = banks.pair()
                S = ps2(b)
                n1 = min(512, keys[1])
                t = mm(S[:, 0:n1], q, k[:, keys[0]:keys[0] + n1], True, True, bw, qw, kw)
                if keys[1] > 512:
                    t = mm(S[:, 512:keys[1]], q, k[:, keys[0] + 512:keys[0] + keys[1]], True, True)
                c = rw.take()
                nm, rs = c[0]
                S = S[:, 0:keys[1]]
                t2_ = dve(lambda e: e.tensor_reduce(nm, S, AX.X, MAX, negate=True), t, c[1])
                p, pw = Pb.take()
                pv = p[:, 0:keys[1]]
                t3 = af(pv, S, ACT.Exp, t2_, pw, bias=nm, accum=rs)
                banks.give_pair(b, t3)
                t4 = recip(dve, rs, rs, t3)
                t5 = ts(dve, pv, pv, rs, None, MUL, None, t4, t3)
                rw.give(c[0], t5)
                st[u] = (p, pv, t5)

            def second(u):
                h, j = units[u]
                p, pv, t = st.pop(u)
                if j == 0:
                    res[h] = PTb.take()
                PT, ptw = res[h]
                b, bw = banks.pair()
                T = ps2(b)
                for k in range(nk):
                    last = tr(T[:, k * 128:(k + 1) * 128], pv[:, k * 128:(k + 1) * 128], 128, t, bw)
                Pb.give(p, last)
                dst = PT[:, 0:nk, j * 128:(j + 1) * 128]
                src_ = T[:, 0:nk * 128].rearrange("p (k q) -> p k q", q=128)
                if u % 2:
                    t = af(dst, src_, ACT.Copy, last, ptw)
                else:
                    t = cp(dve, dst, src_, last, ptw)
                banks.give_pair(b, t)
                st[h, "pt"] = st.get((h, "pt"), []) + [t]
                if j == nq - 1:
                    o, r0, ow = ov(h)
                    b, bw = banks.take()
                    rows = slice(r0, r0 + 64)
                    for k in range(nk):
                        v, vw = vv(k, h)
                        last = mm(ps(b, nq * 128, rows), v, PT[:, k, 0:nq * 128], k == 0, k == nk - 1,
                                  bw, vw, st[h, "pt"])
                    PTb.give(PT, last)
                    t = cp(dve, o, ps(b, nq * 128, rows), last, ow)
                    banks.give(b, t)
                    res[h, "o"] = t

            for i in range(len(units) + 2):
                if i < len(units):
                    first(i)
                if i >= 2:
                    second(i - 2)
                step()
            return {h: res[h, "o"] for h in heads}

        red = Ring([(SM[:, 620 + 2 * i:621 + 2 * i], SM[:, 621 + 2 * i:622 + 2 * i]) for i in range(8)])
        s_turn = P.sem("s_turn")

        S5 = {}

        def s5_tables():
            pw = WR[:, 4, 1536:2048].rearrange("p (n v) -> p n v", v=16)
            nx = [0]

            def new():
                nx[0] += 1
                return pw[:, nx[0] - 1, :]

            cs = [(new(), new()) for _ in range(9)]
            mag, zre, zim = col("mag", 16), col("zre", 16), col("zim", 16)
            t = [None]

            def o(fn):
                t[0] = dve(fn, t[0])

            def s_(out_, i0, s1, s2, o0, o1=None):
                if o1 is None:
                    o(lambda e: e.tensor_scalar(out_, i0, s1, None, o0))
                else:
                    o(lambda e: e.tensor_scalar(out_, i0, s1, s2, o0, o1))

            def v_(out_, i0, i1, op):
                o(lambda e: e.tensor_tensor(out_, i0, i1, op))

            def f_(out_, i0, s, i1, o0, o1):
                o(lambda e: e.scalar_tensor_tensor(out=out_, in0=i0, scalar=s, in1=i1, op0=o0, op1=o1))

            def copy(out_, i0):
                o(lambda e: e.tensor_copy(out_, i0))

            def series(out_, z, cs_):
                s_(out_, z, cs_[-1], 1.0, MUL, ADD)
                for c in cs_[-2::-1]:
                    v_(out_, out_, z, MUL)
                    s_(out_, out_, c, 1.0, MUL, ADD)

            A, B, C, E_, F_, G_, I_ = (new() for _ in range(7))
            t[0] = ts(dve, A, dt, -87.0, 87.0, MAX, MIN, K, [tk for tk in trow[:0]])
            s_(B, A, 1.4426950408889634, None, MUL)
            Ii = I_.bitcast(I32)
            copy(Ii, B)
            copy(B, Ii)
            f_(A, B, -0.693359375, A, MUL, ADD)
            f_(A, B, 2.12194440e-4, A, MUL, ADD)
            series(C, A, [1.0, 1 / 2, 1 / 3, 1 / 4, 1 / 5, 1 / 6, 1 / 7])
            s_(B, B, 127.0, 8388608.0, ADD, MUL)
            copy(Ii, B)
            v_(A, C, I_, MUL)
            s_(B, lre, -1e-4, None, MIN)
            v_(C, B, A, MUL)
            s_(C, C, -80.0, 1.0 / 256, MAX, MUL)
            series(E_, C, [1 / 2, 1 / 3, 1 / 4, 1 / 5, 1 / 6, 1 / 7])
            v_(E_, E_, C, MUL)
            for _ in range(8):
                s_(C, E_, 2.0, None, ADD)
                v_(E_, E_, C, MUL)
            s_(mag, E_, 1.0, None, ADD)
            v_(A, A, lim, MUL)
            s_(C, A, 0.15915494309189535, None, MUL)
            copy(Ii, C)
            copy(C, Ii)
            f_(A, C, -6.28125, A, MUL, ADD)
            f_(A, C, -0.0019350051879882812, A, MUL, ADD)
            f_(A, C, -3.0199160501e-07, A, MUL, ADD)
            s_(A, A, 0.5, None, MUL)
            v_(C, A, A, MUL)
            series(F_, C, [-1 / 6, -1 / 20, -1 / 42, -1 / 72, -1 / 110, -1 / 156])
            v_(F_, F_, A, MUL)
            series(G_, C, [-1 / 2, -1 / 12, -1 / 30, -1 / 56, -1 / 90, -1 / 132, -1 / 182])
            v_(C, F_, F_, MUL)
            s_(C, C, -2.0, None, MUL)
            s_(cs[0][0], C, 1.0, None, ADD)
            f_(cs[0][1], F_, 2.0, G_, MUL, MUL)
            f_(A, E_, 1.0, C, ADD, MUL)
            v_(A, A, E_, ADD)
            v_(C, mag, cs[0][1], MUL)
            v_(F_, B, B, MUL)
            v_(G_, lim, lim, MUL)
            v_(F_, F_, G_, ADD)
            o(lambda e: e.reciprocal(F_, F_))
            v_(G_, A, B, MUL)
            v_(I_, C, lim, MUL)
            v_(G_, G_, I_, ADD)
            v_(zre, G_, F_, MUL)
            v_(G_, C, B, MUL)
            v_(I_, A, lim, MUL)
            v_(G_, G_, I_, SUB)
            v_(zim, G_, F_, MUL)
            for j in range(8):
                c, s = cs[j]
                v_(A, s, s, MUL)
                s_(cs[j + 1][0], A, -2.0, 1.0, MUL, ADD)
                f_(cs[j + 1][1], s, 2.0, c, MUL, MUL)
            S5["p"] = t[0]
            E_ = WR[:, 4, 0:1024].rearrange("p (a n) -> p a n", n=512)
            T_ = WR[:, 4, 1024:1536].rearrange("p (a n) -> p a n", n=256)
            sd = P.sem("s_tab")
            S5["d"] = []
            td = None
            for r in range(16):
                tc_ = fill(pool, E_[:, 0, 0:1], 1.0, td)
                tq = fill(pool, E_[:, 1, 0:1], 0.0, td)
                for j in range(9):
                    n = 1 << j
                    c, s = cs[j][0][:, r:r + 1], cs[j][1][:, r:r + 1]
                    t1_ = ts(pool, T_[:, :, 0:n], E_[:, :, 0:n], s, None, MUL, None, tc_, tq, S5["p"])
                    t2_ = ts(pool, E_[:, :, n:2 * n], E_[:, :, 0:n], c, None, MUL, None)
                    tc_ = tt(pool, E_[:, 0, n:2 * n], E_[:, 0, n:2 * n], T_[:, 1, 0:n], SUB, t1_, t2_)
                    tq = tt(pool, E_[:, 1, n:2 * n], E_[:, 1, n:2 * n], T_[:, 0, 0:n], ADD, t1_, t2_)
                td = P.dma(sp, sd, EDR[r], E_.rearrange("p a n -> p (a n)"), tc_, tq)
                S5["d"].append(td)
                yield

        if "l0" in parts:
            ada1(0, 0, 8)
            modulate(0, 0, (0, 1))
            fence = P.fence()
            q_ = arena(0, 8, TOK)
            k_ = arena(6144, 4, TOK)
            V_ = arena(9216, 6, 256)
            Pbuf = [arena(10752 + i * 768, 768) for i in range(3)]
            PTbuf = [arena(13056 + i * 3072, 6, 512) for i in range(2)]
            TURN = arena(19200, 2, 512)
            tturn = [P.dma(sp, s_turn, TURN, a["k_turn"][0:2].rearrange("a p n -> p a n"), fence)]
            tmps = tmp_ring(20224, 8, fence)
            qt_, kt_, vt_ = {}, {}, {}

            def norm_rope(dsts, s, b, t, gain, scale, store):
                n = SEG[s][1]
                raw, w1 = tmps.take()
                sq, w2 = tmps.take()
                raw, sq = raw[:, 0:n], sq[:, 0:n]
                t1_ = af(raw, ps(b, n), ACT.Copy, t, w1)
                t2_ = af(sq, ps(b, n), ACT.Square, w2)
                banks.give(b, t2_)
                yield
                b, bw = banks.take()
                t = mm(ps(b, n), mat["head64"], sq, True, True, bw, t2_, K)
                t = af(sq, ps(b, n), ACT.Ln, t, bias=epsc, scale=1.0 / 64)
                banks.give(b, t)
                t = af(sq, sq, ACT.Exp, t, scale=-0.5)
                t = ts(dve, raw, raw, gain, scale, MUL, MUL, t1_, K)
                t = tt(dve, raw, raw, sq, MUL, t, act.last())
                if s == 0:
                    yield
                    b, bw = banks.take()
                    tp = mm(ps(b, n), mat["swap64"], raw, True, True, bw, t, K)
                    tc = tt(pool, raw, raw, TURN[:, 0, :], MUL, t, tturn, tp)
                    t2_ = tt(dve, sq, ps(b, n), TURN[:, 1, :], MUL, tp, tturn, t)
                    banks.give(b, t2_)
                    toks = [tt(dve, dst, raw[r], sq[r], ADD, tc, t2_, fence) for dst, r in dsts]
                else:
                    toks = [cp(dve, dst, raw[r], t, fence) for dst, r in dsts]
                tmps.give(tmp_of[id(w1)], toks)
                tmps.give(tmp_of[id(w2)], toks)
                store(toks)

            tmp_of = {}
            _take = tmps.take

            def take():
                x, w = _take()
                w = list(w)
                tmp_of[id(w)] = x
                keepalive.append(w)
                return x, w
            keepalive = []
            tmps.take = take

            def evac_qkv(m, s, b, t):
                if m < 8:
                    r = slice(0, 128)
                    return norm_rope([(seg(q_, m, s), r)], s, b, t, qg, 0.125,
                                     lambda tk: qt_.setdefault((m, s), []).extend(tk))
                m -= 8
                lo, hi = slice(0, 64), slice(64, 128)
                o0, n = SEG[s]
                d = [(k_[lo, 2 * m, o0:o0 + n], lo), (k_[hi, 2 * m + 1, o0:o0 + n], hi)]

                def store(tk):
                    t1_ = cp(dve, k_[hi, 2 * m, o0:o0 + n], k_[lo, 2 * m, o0:o0 + n], tk)
                    t2_ = cp(dve, k_[lo, 2 * m + 1, o0:o0 + n], k_[hi, 2 * m + 1, o0:o0 + n], tk)
                    kt_[2 * m, s] = tk + [t1_]
                    kt_[2 * m + 1, s] = tk + [t2_]
                return norm_rope(d, s, b, t, kg, 1.0, store)

            linear(a["gqa_w_qkv"][0], tiles(0, 10), [8], hrhs, (0, 1), evac_qkv)

            token_major(a["gqa_w_qkv"][0], 1280, 256, lambda j: V_[:, j, :], vt_, 6, fence)
            drain()
            hfence = pe.last()
            Pb, PTb = Ring(Pbuf), Ring(PTbuf)
            ot = {}

            def q_view(h, j):
                r = slice(64 * (h % 2), 64 * (h % 2) + 64)
                return q_[r, h // 2, j * 128:(j + 1) * 128], qt_[h // 2, 0 if j < 4 else 1]

            def k_view(h):
                r = slice(64 * (h % 2), 64 * (h % 2) + 64)
                return k_[r, h // 4, :], kt_[h // 4, 0] + kt_[h // 4, 1]

            def v_view(base):
                return lambda k, h: (V_[:, base + k, (h // 4) * 64:(h // 4) * 64 + 64], vt_[base + k])

            def o_view(s):
                def o(h):
                    r0 = 64 * (h % 2)
                    return H[r0:r0 + 64, h // 2, SEG[s][0]:SEG[s][0] + SEG[s][1]], r0, hfence
                return o

            o1 = attention(range(16), q_view, k_view, v_view(0), o_view(0), [0, 1, 2, 3], (0, 768), Pb, PTb, red, "a")
            o2 = attention(range(16), q_view, k_view, v_view(4), o_view(1), [4, 5], (512, 256), Pb, PTb, red, "c")
            for f in range(8):
                ht[f, 0] = [o1[2 * f], o1[2 * f + 1]]
                ht[f, 1] = [o2[2 * f], o2[2 * f + 1]]
            ada1(0, 8, 24)
            linear(a["gqa_w_o"][0], tiles(0, 8), [8], hrhs, (0, 1), add_gated(0, 0))

        def mlp(i, segs):
            tm = tmp_ring(0, 4, P.fence())
            layer_norm(2 * i, segs, tm)
            modulate(i, 1, segs, pe.last())
            fence = P.fence()
            hid = arena(0, 32, TOK)
            hidt = {}

            def evac(m, s, b, t):
                t = af(seg(hid, m, s), ps(b, SEG[s][1]), ACT.Relu, t, fence)
                t = stt(seg(hid, m, s), ps(b, SEG[s][1]), 0.0, seg(hid, m, s), MAX, MUL, t)
                banks.give(b, t)
                hidt[m, s] = [t]

            if i == 0:
                side.append(s5_tables())
            linear(a["mlp_w1"][i], tiles(0, 32), [8], hrhs, segs, evac)
            linear(a["mlp_w2"][i], tiles(0, 8), [8, 8, 8, 8], lambda k, s: (seg(hid, k, s), hidt[k, s]), segs,
                   add_gated(i, 1))
            tm = tmp_ring(0, 4, P.fence())
            layer_norm(2 * i + 1, segs, tm)

        if "l0" in parts:
            mlp(0, (0, 1))

        if "l1" in parts:
            ada1(1, 0, 24)
            modulate(1, 0, (0, 1), pe.last())
            fence = P.fence()
            cq = arena(0, 3, 512)
            ckv = arena(1536, 2, TOK)
            kpe = arena(3072, 768)
            grp = [(arena(3840 + g * 6656, 4, TOK), arena(6912 + g * 6656, 4, 512), arena(8960 + g * 6656, 6, 256))
                   for g in range(2)]
            Pbuf = [arena(17152 + i * 768, 768) for i in range(3)]
            PTbuf = [arena(19456, 6, 512)]
            tmps = tmp_ring(22528, 2, fence)
            TURN = EB[:, 0:1024].rearrange("p (a n) -> p a n", n=512)
            tturn = [P.dma(sp, s_turn, TURN, a["k_turn"][2:4].rearrange("a p n -> p a n"), fence)]
            ct = {}
            W_IN = a["mla_w_in"][0]

            def evac_c(m, s, b, t):
                if m < 3 and s == 1:
                    raise AssertionError
                dst = cq[:, m, :] if m < 3 else seg(ckv, m - 3, s)
                t = af(dst, ps(b, SEG[s][1]), ACT.Copy, t, fence)
                banks.give(b, t)
                ct[m, s] = [t]

            linear(W_IN, tiles(0, 3), [8], hrhs, (0,), evac_c)
            linear(W_IN, [(384, 256, [(3, 0, 128), (4, 128, 128)])], [8], hrhs, (0, 1), evac_c)
            r96, rp = slice(0, 96), slice(64, 96)
            kpt = {}

            def rope96(b, n, t, dst, lat, scale, store, only_pe):
                x, w1 = tmps.take()
                if not lat:
                    t = af(dst[rp, :], ps(b, n, rp), ACT.Copy, t, fence)
                    banks.give(b, t)
                    tmps.give(x, w1)
                    store([t])
                    return
                t = af(x[r96, :], ps(b, n, r96), ACT.Copy, t, w1, scale=scale)
                banks.give(b, t)
                b, bw = banks.take()
                tp = mm(ps(b, n, r96), mat["swap96"][r96, 0:96], x[r96, :], True, True, bw, t, K)
                y, w2 = tmps.take()
                ty = tt(dve, y[r96, :], ps(b, n, r96), TURN[r96, 1, :], MUL, tp, w2, tturn)
                banks.give(b, ty)
                tx = tt(pool, x[r96, :], x[r96, :], TURN[r96, 0, :], MUL, tp, tturn)
                rows = rp if only_pe else r96
                t = tt(dve, dst[rows, :], x[rows, :], y[rows, :], ADD, tx, ty, fence)
                tmps.give(x, t)
                tmps.give(y, t)
                store([t])

            def evac_kpe(m, s, b, t):
                o0, n = SEG[s]
                rope96(b, n, t, kpe[:, o0:o0 + n], s == 0, 1.0, lambda tk: kpt.__setitem__(s, tk), True)

            linear(W_IN, [(576, 96, [(0, 0, 96)])], [8], hrhs, (0, 1), evac_kpe)
            hfence = pe.last()

            def rms(src, n_t, s, gains, scale, toks, o):
                n = SEG[s][1]
                b, bw = banks.take()
                for f in range(n_t):
                    tmp, tw = tmps.take()
                    t = af(tmp[:, 0:n], src(f), ACT.Square, toks[f], tw)
                    last = mm(ps(b, n), mat["ones"], tmp[:, 0:n], f == 0, f == n_t - 1, bw, t, K)
                    tmps.give(tmp, last)
                tr_ = rstd(b, n, scale, last, o)
                res = []
                for f in range(n_t):
                    res.append([stt(src(f), src(f), gains[:, f:f + 1], STAT[o][:, 0:n], MUL, MUL, tr_, toks[f])])
                statt[o] = res[-1]
                return res

            r_ = rms(lambda f: cq[:, f, :], 3, 0, mqg, 1.0 / 384, [ct[f, 0] for f in range(3)], 0)
            for f in range(3):
                ct[f, 0] = r_[f]
            for s in (0, 1):
                r_ = rms(lambda f: seg(ckv, f, s), 2, s, mkg, 1.0 / 256, [ct[3 + f, s] for f in range(2)], 1 + s)
                for f in range(2):
                    ct[3 + f, s] = r_[f]
            Pb, PTb = Ring(Pbuf), Ring(PTbuf)
            gfree = [[], []]
            oall = {}
            for g in range(4):
                kT, qT, Vg = grp[g % 2]
                gw = gfree[g % 2]
                qt_, kt_, vt_ = {}, {}, {}

                def evac_q(m, s, b, t):
                    rope96(b, 512, t, qT[:, m, :], True, 96.0 ** -0.5, lambda tk: qt_.__setitem__(m, tk), False)
                fence_, fence = fence, fence + gw
                linear(a["mla_w_uq"][0], [(g * 384, 384, [(m, m * 96, 96) for m in range(4)])], [3],
                       lambda k, s: (cq[:, k, :], ct[k, 0]), (0,), evac_q)
                slot, v, t = weights(a["mla_w_ukv"][0][:, g * 512:(g + 1) * 512], 2, 512)
                for m in range(4):
                    for s in (0, 1):
                        n = SEG[s][1]
                        b, bw = banks.take()
                        for k in range(2):
                            last = mm(ps(b, n, slice(0, 64)), v[:, k, m * 128:m * 128 + 64], seg(ckv, k, s),
                                      k == 0, k == 1, bw, t, ct[3 + k, s])
                        d = kT[0:64, m, SEG[s][0]:SEG[s][0] + n]
                        tk = af(d, ps(b, n, slice(0, 64)), ACT.Copy, last, fence)
                        banks.give(b, tk)
                        kt_.setdefault(m, []).append(tk)
                    tk = af(kT[rp, m, :], kpe[rp, :], ACT.Copy, kpt[0], kpt[1], fence)
                    kt_[m].append(tk)
                for j in range(6):
                    b, bw = banks.take()
                    for k in range(2):
                        r = v[:, k, :].rearrange("p (m c) -> p m c", c=128)[:, :, 64:128]
                        last = mm(ps(b, 256).rearrange("p (m c) -> p m c", c=64), ckv[:, k, j * 128:(j + 1) * 128], r,
                                  k == 0, k == 1, bw, t, ct[3 + k, 0 if j < 4 else 1])
                    tk = af(Vg[:, j, :], ps(b, 256), ACT.Copy, last, fence)
                    banks.give(b, tk)
                    vt_[j] = [tk]
                wring.give(slot, last)

                def o_view(m, g=g):
                    h = 4 * g + m
                    r0 = 64 * (h % 2)
                    return H[r0:r0 + 64, h // 2, 0:512], r0, hfence
                o = attention(range(4), lambda m, j: (qT[r96, m, j * 128:(j + 1) * 128], qt_[m]),
                              lambda m: (kT[r96, m, :], kt_[m]),
                              lambda k, m: (Vg[:, k, m * 64:(m + 1) * 64], vt_[k]),
                              o_view, [0, 1, 2, 3], (0, 768), Pb, PTb, red, "m")
                for m in range(4):
                    oall[4 * g + m] = o[m]
                gfree[g % 2] = pe.last()
                fence = fence_
            for f in range(8):
                ht[f, 0] = [oall[2 * f], oall[2 * f + 1]]
            linear(a["mla_w_o"][0], tiles(0, 8), [8], hrhs, (0,), add_gated(1, 0))
            mlp(1, (0,))

        drain()
        if "mix" in parts and not S5:
            for _ in s5_tables():
                pass
        if "mix" in parts or "ffn" in parts:
            ada(a["ada_w_2"][0], 1, 2, adb2, MOD2.unsqueeze(2), (1, 2, 4, 5), 0, 24, "b2")

        def rms_mod(w, j, tmps, hw):
            G = col("G", 8)
            tg = tt(dve, G, w, MOD2[:, (3 * j + 1) * 8:(3 * j + 2) * 8], MUL, modt["b2"], K, dve.last())
            b, bw = banks.take()
            for f in range(8):
                tmp, tw = tmps.take()
                t = af(tmp, seg(X, f, 0), ACT.Square, xt[f, 0], tw)
                last = mm(ps(b), mat["ones"], tmp, f == 0, f == 7, bw, t, K)
                tmps.give(tmp, last)
            tr_ = rstd(b, 512, 1.0 / 1024, last, 0)
            for f in range(8):
                t = stt(seg(H, f, 0), seg(X, f, 0), G[:, f:f + 1], STAT[0], MUL, MUL, tr_, tg, hw)
                ht[f, 0] = [ts(pool if f % 2 else dve, seg(H, f, 0), seg(H, f, 0), MOD2[:, 3 * j * 8 + f:3 * j * 8 + f + 1],
                               None, ADD, None, t)]
            statt[0] = [t]

        def add_rms(Y, yt, w, j, tmps):
            G = col("G2", 8)
            tg = tt(dve, G, w, MOD2[:, (3 * j + 2) * 8:(3 * j + 3) * 8], MUL, modt["b2"], K, dve.last())
            b, bw = banks.take()
            for f in range(8):
                tmp, tw = tmps.take()
                t = af(tmp, Y[:, f, :], ACT.Square, yt[f], tw)
                last = mm(ps(b), mat["ones"], tmp, f == 0, f == 7, bw, t, K)
                tmps.give(tmp, last)
            tr_ = rstd(b, 512, 1.0 / 1024, last, 1)
            for f in range(8):
                t = stt(Y[:, f, :], Y[:, f, :], G[:, f:f + 1], STAT[1], MUL, MUL, tr_, tg)
                xt[f, 0] = [tt(pool if f % 2 else dve, seg(X, f, 0), seg(X, f, 0), Y[:, f, :], ADD, t, xt[f, 0])]
            statt[1] = [t]

        if "mix" in parts:
            HX = [H[:, f, 512:768] for f in range(8)]
            XX = [X[:, f, 512:768] for f in range(8)]

            def blk(fs, buf, i):
                return buf[fs[i // 2]][:, 128 * (i % 2):128 * (i % 2) + 128]

            fence = P.fence()
            gqk, gv = arena(0, 4, 512), arena(2048, 4, 512)
            mqk, mv = arena(4096, 4, 516), arena(6160, 4, 512)
            su = arena(8208, 4, 512)
            gr, mo = arena(10256, 4, 512), arena(12304, 4, 512)
            SO = arena(10256, 4, 768)
            cum, EX = arena(14352, 1024), arena(15376, 1024)
            QKL = Ring([arena(16400, 1024)], fence)
            SD = arena(18448, 4, 512)
            tmps = tmp_ring(20496, 3, fence)
            stm = tmp_ring(22032, 4, fence)
            MSK = AR[:, 24080:24336].bitcast(I8).rearrange("p (l n) -> p l n", n=128)
            s_mx = P.sem("s_mx")
            t = P.dma(sp, P.sem("s_mask"), arena(17424, 1024), a["k_masks"], fence)
            tm = [cp(dve, MSK, arena(17424, 1024).rearrange("p (l n) -> p l n", n=128), t)]
            QKL.give(arena(17424, 1024), tm[0])
            for j in range(2):
                tm.append(P.dma(sp, s_mx, XX[j][0:4, :], a["k_mats"][0:4, 1024 + 256 * j:1280 + 256 * j], fence))
            A2 = XX[3][0:16, :]
            tm.append(P.dma(sp, s_mx, A2, a["gla_a2_2"][0], fence))

            def sel(h):
                return XX[h // 2][0:4, 128 * (h % 2):128 * (h % 2) + 128]

            rms_mod(nrm["pre1_w_2"], 0, tmps, pe.last())
            WI = a["w_in_2"][0]
            tok = {}

            def evac_to(buf, base, name, scale=None, off=0):
                def evac(m, s, b, t):
                    t = af(buf[:, m - base, off:off + 512], ps(b), ACT.Copy, t, fence, scale=scale)
                    banks.give(b, t)
                    tok[name, m - base] = [t]
                return evac

            s_b = P.sem("s_b")

            def s5():
                w0 = stm.take()
                w1 = stm.take()
                w2 = stm.take()
                (x0, f0), (x1, f1), (x2, f2) = w0, w1, w2
                bre, bim = x0[:, 0:256], x0[:, 256:512]
                with_ = [f0, f1, f2]
                tb = [P.dma(sp, s_b, bre.rearrange("p (r c) -> p r c", c=16),
                            a["s5_b_re_2"][0].rearrange("(r g) p c -> (g p) r c", g=2), with_),
                      P.dma(sp, s_b, bim.rearrange("p (r c) -> p r c", c=16),
                            a["s5_b_im_2"][0].rearrange("(r g) p c -> (g p) r c", g=2), with_)]
                BRE, BIM, BTR, BTI = [1, 2], [3, 4], [5, 6], [7, 0]
                CTR, CTI = [4, 5], [6, 7]
                tz = [fill(dve, HX[f], 0.0, fence) for f in (1, 2, 3, 4)]

                def bc(v):
                    return v.unsqueeze(2).to_broadcast([128, 16, 16])

                v3 = lambda x: x.rearrange("p (r c) -> p r c", c=16)
                v4 = lambda x: x.rearrange("p (a r c) -> p a r c", a=2, c=16)
                zr, zi = col("zre", 16), col("zim", 16)
                m = [x1[:, 0:256], x1[:, 256:512], x2[:, 0:256], x2[:, 256:512]]
                q = [tt(dve, v3(m[0]), v3(bre), bc(zr), MUL, tb, S5["p"]),
                     tt(dve, v3(m[1]), v3(bim), bc(zi), MUL, tb),
                     tt(dve, v3(m[2]), v3(bim), bc(zr), MUL, tb),
                     tt(dve, v3(m[3]), v3(bre), bc(zi), MUL, tb)]
                tb2 = []
                for g in range(2):
                    r = slice(64 * g, 64 * g + 64)
                    for fs, p0, p1, op in ((BRE, 0, 1, SUB), (BIM, 2, 3, ADD)):
                        for i in range(2):
                            d = HX[fs[i]][r, :].rearrange("p (r c) -> p r c", c=32)[:, :, 16 * g:16 * g + 16]
                            tb2.append(tt(dve, d, v4(m[p0])[r, i], v4(m[p1])[r, i], op, q, tz))
                stm.give(x0, tb2)
                stm.give(x1, tb2)
                stm.give(x2, tb2)
                yield
                tbt = []
                for src, dst in ((BRE, BTR), (BIM, BTI)):
                    b, bw = banks.take()
                    for i in range(4):
                        last = tr(PS[:, b, i * 128:(i + 1) * 128], blk(src, HX, i), 128, tb2, bw)
                    for i in range(2):
                        t = cp(dve, HX[dst[i]], PS[:, b, i * 256:(i + 1) * 256],
                                last, fence)
                    tbt.append(t)
                    banks.give(b, t)
                    yield
                tct = []
                for name, dst, sign in (("s5_c_re_2", CTR, 1.0), ("s5_c_im_2", CTI, -1.0)):
                    x, w = stm.take()
                    xv = x.rearrange("p (i n) -> p i n", n=128)
                    src = a[name][0].rearrange("(i g) c p -> (g c) i p", g=8)
                    s_c = P.sem("s_" + name)
                    tcl = [P.dma(sp, s_c, xv[:, :, 64 * g:64 * g + 64], src, w) for g in range(2)]
                    yield
                    b, bw = banks.take()
                    for i in range(4):
                        last = tr(PS[:, b, i * 128:(i + 1) * 128], xv[:, i, :], 128, tcl, bw)
                    for i in range(4):
                        t = stt(blk(dst, XX, i), PS[:, b, i * 128:(i + 1) * 128], sign, mat["cmask"], MUL, MUL, last, fence)
                    stm.give(x, last)
                    banks.give(b, t)
                    tct.append(t)
                    yield
                s_e = [P.sem("s_e0"), P.sem("s_e1")]
                ering = Ring([0, 1], fence)
                mag = col("mag", 16)
                for i in range(4):
                    yb, ybw = banks.take()
                    for qd in range(4):
                        r = 4 * i + qd
                        e_, ew = ering.take()
                        EV = EB[:, e_ * 1024:(e_ + 1) * 1024]
                        te = P.dma(sp, s_e[e_], EV, EDR[r], ew, S5["d"][r])
                        co, si = EV[:, 0:512], EV[:, 512:1024]
                        rows = slice(32 * qd, 32 * qd + 32)
                        b0, bw0 = banks.take()
                        b1, bw1 = banks.take()
                        l0 = mm(ps(b0), blk(BTR, HX, i)[rows, :], su[rows, i, :], True, True, bw0, tbt, tok["su", i])
                        l1 = mm(ps(b1), blk(BTI, HX, i)[rows, :], su[rows, i, :], True, True, bw1)
                        ms = [stm.take() for _ in range(4)]
                        (m1, v1), (m2, v2), (m3, v3_), (m4, v4_) = ms
                        t1_ = tt(dve, m1, ps(b0), co, MUL, l0, te, v1)
                        t4_ = tt(dve, m4, ps(b0), si, MUL, v4_)
                        banks.give(b0, t4_)
                        t2_ = tt(dve, m2, ps(b1), si, MUL, l1, v2)
                        t3_ = tt(dve, m3, ps(b1), co, MUL, v3_)
                        banks.give(b1, t3_)
                        ta = tt(pool, m1, m1, m2, ADD, t1_, t2_)
                        tb_ = tt(pool, m3, m3, m4, SUB, t3_, t4_)
                        yield
                        mg = mag[:, r:r + 1].to_broadcast([128, 512])
                        t2_ = scan(dve, m2, mg, m1, 0.0, MUL, ADD, ta)
                        t4_ = scan(dve, m4, mg, m3, 0.0, MUL, ADD, tb_)
                        t1_ = tt(dve, m1, m2, co, MUL, t2_)
                        t3_ = tt(pool, m3, m4, si, MUL, t4_)
                        tx = tt(pool, m1, m1, m3, SUB, t1_, t3_)
                        t3_ = tt(pool, m3, m2, si, MUL, tx)
                        t4_ = tt(dve, m4, m4, co, MUL, t3_)
                        ty = tt(pool, m3, m3, m4, ADD, t3_, t4_)
                        ering.give(e_, ty)
                        yield
                        last = mm(PS[rows, yb, :], blk(CTR, XX, i)[:, rows], m1, True, False, tx, ybw, tct)
                        last = mm(PS[rows, yb, :], blk(CTI, XX, i)[:, rows], m3, False, True, ty)
                        for x in (m1, m2, m3, m4):
                            stm.give(x, last)
                        yield
                    (y, w0_), (z, w1_) = stm.take(), stm.take()
                    t = stt(y, su[:, i, :], s5d[:, i:i + 1], ps(yb), MUL, ADD, last, w0_, K)
                    banks.give(yb, t)
                    t = tt(dve, z, y, y, MUL, t, w1_)
                    t = ts(dve, z, z, 0.044715, 1.0, MUL, ADD, t)
                    t = tt(dve, z, z, y, MUL, t)
                    t = af(z, z, ACT.Exp, t, scale=-2.0 * 0.7978845608028654)
                    t = ts(dve, z, z, 1.0, None, ADD, None, t)
                    t = recip(dve, z, z, t)
                    t = tt(dve, su[:, i, :], y, z, MUL, t)
                    stm.give(y, t)
                    stm.give(z, t)
                    tok["ys", i] = [t]
                    yield

            GA, gaw = tmps.take()
            got = {}

            def evac_ga(m, s, b, t):
                got["ga"] = af(GA[0:16, :], ps(b, 512, slice(0, 16)), ACT.Copy, t, gaw)
                banks.give(b, got["ga"])

            linear(WI, [(1024, 16, [(0, 0, 16)])], [8], hrhs, (0,), evac_ga)
            linear(WI, tiles(3096, 4), [8], hrhs, (0,), evac_to(su, 0, "su"))
            side.append(s5())

            def log_sigmoid(rows, z, tmp, t):
                t1_ = stt(tmp[rows, :], z[rows, :], -1.0, z[rows, :], MUL, MAX, t)
                t1_ = af(tmp[rows, :], tmp[rows, :], ACT.Exp, t1_, scale=-1.0)
                t1_ = af(tmp[rows, :], tmp[rows, :], ACT.Ln, t1_, K, bias=onec[rows, :])
                return stt(z[rows, :], z[rows, :], 0.0, tmp[rows, :], MIN, SUB, t1_)

            tcum = []
            allr = slice(0, 128)
            for m in range(2):
                b, bw = banks.take()
                last = mm(ps(b), A2[:, m * 128:(m + 1) * 128], GA[0:16, :], True, True, bw, got["ga"], tm)
                (z, w0_), (y, w1_) = tmps.take(), tmps.take()
                t = ts(dve, z, ps(b), glab[:, m:m + 1], None, ADD, None, last, w0_, K)
                banks.give(b, t)
                t = log_sigmoid(allr, z, y, [t, w1_])
                t = scan(dve, cum[:, m * 512:(m + 1) * 512], onec.to_broadcast([128, 512]), z, 0.0, MUL, ADD, t, fence)
                tcum.append(t)
                tmps.give(z, t)
                tmps.give(y, t)
            tmps.give(GA, last)

            def evac_gqk(m, s, b, t):
                t = af(gqk[:, m, :], ps(b), ACT.Copy, t, fence, scale=0.125 if m < 2 else 1.0)
                banks.give(b, t)
                tok["gqk", m] = [t]

            linear(WI, tiles(0, 4), [8], hrhs, (0,), evac_gqk)
            for c in range(2):
                tk = {}
                token_major(WI, 512 + 256 * c, 256, lambda j: gv[:, j, 256 * c:256 * c + 256], tk, 4, fence)
                for j in range(4):
                    tok.setdefault(("gv", j), []).extend(tk[j])
            tqk = [tok["gqk", m] for m in range(4)]
            GQ, GK = (arena(o_, 1024) for o_ in (0, 1024))
            tsd = fill(dve, SD.rearrange("p a n -> p (a n)"), 0.0, fence)
            tso = {}

            def gla_level(lv, h):
                if h:
                    nb = 512 // h
                    L = lambda x: x.rearrange("p (b c) -> p b c", c=2 * h)
                    ref = L(cum)[:, :, h - 1:h].to_broadcast([128, nb, h])
                    t1_ = tt(dve, L(EX)[:, :, 0:h], ref, L(cum)[:, :, 0:h], SUB, tcum, got.get("ex"))
                    t2_ = tt(dve, L(EX)[:, :, h:2 * h], L(cum)[:, :, h:2 * h], ref, SUB)
                    t = af(EX, EX, ACT.Exp, t1_, t2_, scale=1.0 / 16)
                    qk, w = QKL.take()
                    t1_ = tt(dve, L(qk)[:, :, 0:h], L(EX)[:, :, 0:h], L(GK)[:, :, 0:h], MUL, t, w, tqk)
                    t2_ = tt(pool, L(qk)[:, :, h:2 * h], L(EX)[:, :, h:2 * h], L(GQ)[:, :, h:2 * h], MUL, t, w, tqk)
                    got["ex"] = [t1_, t2_]
                    lt, rt, tw = qk, qk, [t1_, t2_]
                else:
                    lt, rt, tw = GK, GQ, tqk
                for hd in range(4):
                    r, o_ = slice(64 * (hd % 2), 64 * (hd % 2) + 64), 512 * (hd // 2)
                    b, bw = banks.take()
                    if h >= 128:
                        jobs = [(0, 256, 256, 128), (1, 256, 256, 384)] if h == 256 else [(0, 128, 128, 0), (2, 384, 128, 640)]
                        for n_, (s, t0, n, so) in enumerate(jobs):
                            last = mm(PS[:, b, n_ * 256:n_ * 256 + n], lt[r, o_ + s * 128:o_ + s * 128 + 128],
                                      rt[r, o_ + t0:o_ + t0 + n], True, True, bw, tw)
                        for n_, (s, t0, n, so) in enumerate(jobs):
                            t = af(SO[:, hd, so:so + n], PS[:, b, n_ * 256:n_ * 256 + n], ACT.Copy, last, fence)
                        tso.setdefault(hd, []).append(t)
                    else:
                        for s in range(4):
                            x = o_ + s * 128
                            last = mm(PS[:, b, s * 128:s * 128 + 128], lt[r, x:x + 128], rt[r, x:x + 128], True, True, bw, tw)
                        mk = MSK[:, lv, :].unsqueeze(1).to_broadcast([128, 4, 128])
                        sd = SD[:, hd, :].rearrange("p (a n) -> p a n", n=128)
                        t = cpred(dve, sd, mk, ps(b).rearrange("p (a n) -> p a n", n=128), last, tsd, tm, tso.get(("d", hd)))
                        tso["d", hd] = [t]
                    banks.give(b, t)
                if h:
                    QKL.give(qk, last)

            for h in (256, 128):
                gla_level(None, h)
                step()
            for lv, h in enumerate((64, 32, 16, 8, 4, 2, 1, 0)):
                gla_level(lv, h)
                step()
            gfence = P.fence()
            OG = gqk
            tog = {}
            for hd in range(4):
                b, bw = banks.take()
                w = [tso[hd], tso["d", hd], bw]
                for s in range(4):
                    v = gv[:, s, hd * 128:hd * 128 + 128]
                    w.append(tok["gv", s])
                    last = mm(PS[:, b, s * 128:s * 128 + 128], v, SD[:, hd, s * 128:s * 128 + 128], s == 0, s == 3, w)
                    if s < 3:
                        so = (0, 384, 640)[s]
                        last = mm(PS[:, b, (s + 1) * 128:512], v, SO[:, hd, so:so + 384 - 128 * s], False, False)
                t = af(OG[:, hd, :], ps(b), ACT.Copy, last, gfence)
                banks.give(b, t)
                x, xw = tmps.take()
                t2_ = af(x, OG[:, hd, :], ACT.Square, t, xw)
                b, bw = banks.take()
                last = mm(ps(b), mat["ones"], x, True, True, bw, t2_)
                tmps.give(x, last)
                tr_ = rstd(b, 512, 1.0 / 128, last, 0)
                t = stt(OG[:, hd, :], OG[:, hd, :], glanw[:, hd:hd + 1], STAT[0], MUL, MUL, tr_, t)
                statt[0] = [t]
                tog[hd] = [t]
                step()
            gfence = P.fence()

            tz = fill(dve, mqk[:, :, 0:3], 0.0, fence)
            linear(WI, tiles(1552, 4), [8], hrhs, (0,), evac_to(mqk, 0, "mqk", off=3))
            for c in range(2):
                tk = {}
                token_major(WI, 2064 + 256 * c, 256, lambda j: mv[:, j, 256 * c:256 * c + 256], tk, 4, fence)
                for j in range(4):
                    tok.setdefault(("mv", j), []).extend(tk[j])
            slot, w = wring.take()
            v = WR[:, slot, 0:288].rearrange("p (k n) -> p k n", n=36)
            t = fill(dve, v, 0.0, w)
            t = P.dma(sp, wsem[slot], v[:, :, 0:4], WI[:, 2576:2580].rearrange("(k p) n -> p k n", p=128), t)
            t = P.dma(sp, wsem[slot], v[:, :, 32:36], WI[:, 2580:2584].rearrange("(k p) n -> p k n", p=128))
            gb, bw = banks.take()
            for k in range(8):
                last = mm(ps(gb, 512, slice(0, 36)), v[:, k, :], H[:, k, 0:512], k == 0, k == 7, t, bw, ht[k, 0])
            wring.give(slot, last)
            (x0, f0), (x1, f1), (x2, f2) = (tmps.take() for _ in range(3))
            ri, rf = slice(0, 4), slice(32, 36)
            ti = ts(dve, x0[ri, :], ps(gb, 512, ri), ib[ri, :], None, ADD, None, last, f0, K)
            tf = ts(dve, x1[rf, :], ps(gb, 512, rf), ib[rf, :], None, ADD, None, f1)
            banks.give(gb, tf)
            t = log_sigmoid(rf, x1, x2, [tf, f2])
            t = cp(dve, x2[ri, :], x1[rf, :], t)
            BB = EX[ri, 0:512]
            MM = EX[ri, 512:1024]
            t = scan(dve, BB, onec[ri, :].to_broadcast([4, 512]), x2[ri, :], 0.0, MUL, ADD, t, gfence)
            ta = tt(dve, x0[ri, :], x0[ri, :], BB, SUB, t, ti)
            tM = scan(dve, MM, x0[ri, :], x0[ri, :], 0.0, MAX, MAX, ta)
            t = tt(dve, x2[ri, :], BB, MM, ADD, tM)
            tem = af(x2[ri, :], x2[ri, :], ACT.Exp, t, scale=-1.0)
            b, bw = banks.take()
            for s in range(4):
                last = tr(PS[:, b, 4 * s:4 * s + 4], x0[ri, s * 128:(s + 1) * 128], 4, ta, bw)
            acol = col("acol", 16)
            tac = cp(dve, acol, PS[:, b, 0:16], last)
            banks.give(b, tac)
            tmps.give(x1, tac)
            tmps.give(x0, tac)
            mc = arena(14352, 2, 512)
            mcs = [mc[:, 0, :], mc[:, 1, :], arena(16400, 512), arena(16912, 512)]
            ex = arena(17424, 512)
            tmc = {}
            for m in range(4):
                y = mcs[m]
                t = ts(dve, y, mqk[:, m, 0:512], cw[:, 0, m:m + 1], cb[:, m:m + 1], MUL, ADD, tok["mqk", m], tz, gfence, K)
                for j in range(1, 4):
                    t = stt(y, mqk[:, m, j:j + 512], cw[:, j, m:m + 1], y, MUL, ADD, t)
                t = af(ex, y, ACT.Exp, t, got.get("exw"), scale=-1.0)
                t = ts(dve, ex, ex, 1.0, None, ADD, None, t)
                t = recip(dve, ex, ex, t)
                t = stt(y, y, 1.0 if m < 2 else 0.125, ex, MUL, MUL, t)
                got["exw"] = [t]
                tmc[m] = [t]
                step()
            OM = arena(4096, 4, 512)
            PM = SD
            tom = {}
            tpm = gfence
            pfence = P.fence()
            for hd in range(4):
                r = slice(64 * (hd % 2), 64 * (hd % 2) + 64)
                q_, k_ = mcs[hd // 2], mcs[2 + hd // 2]
                bM, bw = banks.take()
                lM = mm(ps(bM), sel(hd), MM, True, True, bw, tM, tm)
                tp = {}
                for s in range(4):
                    n = 512 - 128 * s
                    d = PM[:, s, 128 * s:512]
                    t = ts(dve, d, PS[:, bM, 128 * s:512], acol[:, 4 * s + hd:4 * s + hd + 1], 0.0, SUB, MAX, lM, tac, tpm)
                    if s == 3:
                        banks.give(bM, t)
                    t = af(d, d, ACT.Exp, t, scale=-1.0)
                    b, bw = banks.take()
                    last = mm(PS[:, b, 0:n], k_[r, s * 128:(s + 1) * 128], q_[r, 128 * s:512], True, True, bw,
                              tmc[hd // 2], tmc[2 + hd // 2])
                    t = tt(dve, d, PS[:, b, 0:n], d, MUL, last, t)
                    banks.give(b, t)
                    t = tt(pool, d[:, 0:128], d[:, 0:128], mat["causal"], MUL, t)
                    tp[s] = [t]
                bd, w0_ = banks.take()
                bn, w1_ = banks.take()
                for s in range(4):
                    ld = mm(PS[:, bd, 128 * s:512], mat["ones"], PM[:, s, 128 * s:512], s == 0, s == 3, w0_, tp[s])
                for s in range(4):
                    ln = mm(PS[:, bn, 128 * s:512], mv[:, s, hd * 128:hd * 128 + 128], PM[:, s, 128 * s:512],
                            s == 0, s == 3, w1_, tok["mv", s])
                be, w2_ = banks.take()
                le = mm(ps(be), sel(hd), x2[ri, :], True, True, w2_, tem)
                tpm = [ln]
                x, xw = tmps.take()
                t = af(x, ps(be), ACT.Copy, le, xw)
                banks.give(be, t)
                t = stt(x, ps(bd), -1.0, x, MUL, MAX, t, ld)
                t = tt(dve, x, ps(bd), x, MAX, t)
                banks.give(bd, t)
                t = recip(dve, x, x, t)
                t = tt(dve, OM[:, hd, :], ps(bn), x, MUL, t, ln, pfence)
                banks.give(bn, t)
                tmps.give(x, t)
                tom[hd] = [t]
                step()
            tmps.give(x2, le)
            mfence = P.fence()

            def evac_gr(m, s, b, t):
                x, w = tmps.take()
                t = af(x, ps(b), ACT.Sigmoid, t, w)
                if m < 4:
                    t = tt(dve, x, ps(b), x, MUL, t)
                banks.give(b, t)
                if m < 4:
                    t = tt(pool, OG[:, m, :], OG[:, m, :], x, MUL, t, tog[m])
                    tog[m] = [t]
                else:
                    t = tt(pool, OM[:, m - 4, :], OM[:, m - 4, :], x, MUL, t, tom[m - 4])
                    tom[m - 4] = [t]
                tmps.give(x, t)

            linear(WI, tiles(1040, 4), [8], hrhs, (0,), evac_gr)
            linear(WI, [(c, n, [(m + 4, o_, M) for m, o_, M in ms]) for c, n, ms in tiles(2584, 4)], [8], hrhs, (0,), evac_gr)
            drain()
            YS = gv
            tys = {}

            def evac_glu(m, s, b, t):
                x, w = tmps.take()
                t = af(x, ps(b), ACT.Sigmoid, t, w, K, bias=glub[:, m:m + 1])
                banks.give(b, t)
                t = tt(dve, YS[:, m, :], su[:, m, :], x, MUL, t, mfence)
                tmps.give(x, t)
                tys[m] = [t]

            linear(a["s5_glu_w_2"][0], tiles(0, 4), [4], lambda k, s: (su[:, k, :], tok["ys", k]), (0,), evac_glu)
            mfence = P.fence()
            MG = arena(14352, 8, 512)
            tmg = {}
            sgs = {}
            proj = [(a["proj_gla_2"][0], OG, tog), (a["proj_ml_2"][0], OM, tom), (a["proj_s5_2"][0], YS, tys)]
            tmps = tmp_ring(6160, 8, mfence)
            for mp in range(4):
                for bi, (W, Yb, ty) in enumerate(proj):
                    def evac_z(m, s, b, t, bi=bi):
                        x, w = tmps.take()
                        t = af(x, ps(b), ACT.Sigmoid, t, w, K, bias=bgb[:, bi * 8 + m:bi * 8 + m + 1])
                        banks.give(b, t)
                        sgs[m] = (x, t)

                    def evac_p(m, s, b, t, bi=bi):
                        x, tx = sgs[m]
                        if bi == 0:
                            t = tt(dve, MG[:, m, :], ps(b), x, MUL, t, tx, mfence)
                        else:
                            t = tt(dve, x, ps(b), x, MUL, t, tx)
                        banks.give(b, t)
                        if bi:
                            t = tt(pool, MG[:, m, :], MG[:, m, :], x, ADD, t, tmg[m])
                        tmps.give(x, t)
                        tmg[m] = [t]

                    linear(WI, [(3608 + bi * 1024 + mp * 256, 256, [(2 * mp + j, 128 * j, 128) for j in range(2)])], [8],
                           hrhs, (0,), evac_z)
                    linear(W, [(mp * 256, 256, [(2 * mp + j, 128 * j, 128) for j in range(2)])], [4],
                           lambda k, s, Yb=Yb, ty=ty: (Yb[:, k, :], ty[k]), (0,), evac_p)
            mfence = P.fence()
            Y = arena(0, 8, 512)
            yt = {}

            def evac_y(f, s, b, t):
                t = af(Y[:, f, :], ps(b), ACT.Copy, t, mfence)
                banks.give(b, t)
                yt[f] = [t]

            linear(a["w_out_2"][0], tiles(0, 8), [8], lambda k, s: (MG[:, k, :], tmg[k]), (0,), evac_y)
            add_rms(Y, yt, nrm["post1_w_2"], 0, tmps)
        if "ffn" in parts:
            fence = P.fence()
            hid = arena(0, 22, 512)
            Y = arena(11264, 8, 512)
            tmps = tmp_ring(15360, 8, fence)
            rms_mod(nrm["pre2_w_2"], 1, tmps, pe.last())
            hidt = {}
            W1 = a["ffn_w_in_2"][0]
            for m in range(22):
                slot, w = wring.take()
                v = WR[:, slot, :].rearrange("p (k n) -> p k n", n=256)
                t = P.dma(sp, wsem[slot], v[:, :, 0:128], W1[:, m * 128:(m + 1) * 128].rearrange("(k p) n -> p k n", p=128), w)
                t = P.dma(sp, wsem[slot], v[:, :, 128:256],
                          W1[:, 2816 + m * 128:2816 + (m + 1) * 128].rearrange("(k p) n -> p k n", p=128), w)
                bs = []
                for half in range(2):
                    b, bw = banks.take()
                    for k in range(8):
                        last = mm(ps(b), v[:, k, half * 128:half * 128 + 128], seg(H, k, 0), k == 0, k == 7, bw, t, ht[k, 0])
                    bs.append((b, last))
                wring.give(slot, last)
                (b0, l0), (b1, l1) = bs
                tmp, tw = tmps.take()
                t = af(tmp, ps(b0), ACT.Sigmoid, l0, tw)
                t = tt(dve, tmp, ps(b0), tmp, MUL, t)
                banks.give(b0, t)
                t = tt(dve, hid[:, m, :], ps(b1), tmp, MUL, t, l1, fence)
                banks.give(b1, t)
                tmps.give(tmp, t)
                hidt[m] = [t]
            yt = {}

            def evac_y(f, s, b, t):
                t = af(Y[:, f, :], ps(b), ACT.Copy, t, fence)
                banks.give(b, t)
                yt[f] = [t]
            linear(a["ffn_w_out_2"][0], tiles(0, 8), [8, 8, 6], lambda k, s: (hid[:, k, :], hidt[k]), (0,), evac_y)
            add_rms(Y, yt, nrm["post2_w_2"], 1, tmps)

        s_out = P.sem("s_out")
        fence = P.fence()
        xo = arena(0, 4, 1024)
        for j in range(4):
            tk = []
            for half in range(2):
                b, bw = banks.take()
                for i in range(4):
                    f = half * 4 + i
                    last = tr(PS[:, b, i * 128:(i + 1) * 128], X[:, f, j * 128:(j + 1) * 128], 128, xt[f, 0], bw)
                dst = xo[:, j, half * 512:(half + 1) * 512]
                if half:
                    t = cp(dve, dst, ps(b), last, fence)
                else:
                    t = af(dst, ps(b), ACT.Copy, last, fence)
                banks.give(b, t)
                tk.append(t)
            tout = P.dma(sp, s_out, out[0, j * 128:(j + 1) * 128, :], xo[:, j, :], tk)
        if dbg is not None:
            s_dbg = P.sem("s_dbg")
            tout2 = P.dma(sp, s_dbg, dbg, X[:, :, 512:768], *[xt[f, 1] for f in range(8)] if (0, 1) in xt and "l0" in parts else [P.fence()])
            ends = [tout, tout2]
        else:
            ends = [tout]
        with nc.Block() as block:
            P.emit(block, ends)


INS = ["x", "c", "ctx", "c_ctx", "w_ada", "b_ada", "ln_g", "ln_b", "mlp_w1", "mlp_w2", "gqa_w_qkv", "gqa_q_norm",
       "gqa_k_norm", "gqa_w_o", "mla_w_in", "mla_q_norm", "mla_kv_norm", "mla_w_uq", "mla_w_ukv", "mla_w_o", "c_2",
       "ada_w_2", "ada_b_2", "pre1_w_2", "post1_w_2", "pre2_w_2", "post2_w_2", "w_in_2", "gla_a2_2", "gla_a_b_2",
       "gla_norm_w_2", "ml_conv_w_2", "ml_conv_b_2", "ml_i_b_2", "ml_f_b_2", "s5_lam_re_2", "s5_lam_im_2",
       "s5_log_step_2", "s5_b_re_2", "s5_b_im_2", "s5_c_re_2", "s5_c_im_2", "s5_d_2", "s5_glu_w_2", "s5_glu_b_2",
       "proj_gla_2", "proj_ml_2", "proj_s5_2", "branch_gate_b_2", "w_out_2", "ffn_w_in_2", "ffn_w_out_2"]


def kernel(**inputs):
    import concourse.bacc as bacc
    from concourse.bass_utils import run_bass_kernel_spmd

    nc = bacc.Bacc("TRN2", target_bir_lowering=False, num_devices=1)
    arrays, aps = {}, {}
    given = {n: np.ascontiguousarray(inputs[n]) for n in INS}
    given.update(constants())
    for name, v in given.items():
        arrays["in_" + name] = v
        aps[name] = nc.dram_tensor("in_" + name, v.shape, mybir.dt.from_np(v.dtype), kind="ExternalInput").ap()
    out = nc.dram_tensor("out_0", (1, 512, 1024), F32, kind="ExternalOutput").ap()
    build(nc, aps, out)
    r = run_bass_kernel_spmd(nc, [arrays], core_ids=[0])
    return r.results[0]["out_0"]
```

```python
from contextlib import ExitStack

import numpy as np

import concourse.bass as bass
from concourse import mybir

F32 = mybir.dt.float32
I8 = mybir.dt.uint8
BF = mybir.dt.bfloat16
I32 = mybir.dt.int32
ALU = mybir.AluOpType
ACT = mybir.ActivationFunctionType
AX = mybir.AxisListType
D = 1024
LAT, CTX = 512, 256
TOK = LAT + CTX
SEG = [(0, LAT), (LAT, CTX)]
ALPHA = (2.0 * 2) ** 0.25
EPS = 1e-6
PI = float(np.pi)


class Token:

    def __init__(self, eng, n):
        self.eng, self.n, self.value = eng, n, None


class DmaToken:
    def __init__(self, sem, value):
        self.sem, self.value = sem, value


class Queue:

    def __init__(self, name):
        self.name, self.ops, self.sem = name, [], None

    def __call__(self, fn, *waits, at=None):
        t = Token(self, 0)
        (self.ops if at is None else at).append((flat(waits), fn, t, None))
        return t

    def place(self):
        self.ops.append([])
        return self.ops[-1]

    def last(self):
        return next(([o[2]] for o in reversed(self.ops) if isinstance(o, tuple)), [])

    def close(self):
        self.ops = [x for o in self.ops for x in (o if isinstance(o, list) else [o])]


def flat(x):
    if x is None:
        return []
    if isinstance(x, (list, tuple)):
        return [z for y in x for z in flat(y)]
    return [x]


class Program:
    def __init__(self, nc, ctx):
        self.nc, self.ctx = nc, ctx
        self.pe, self.act, self.dve, self.pool, self.sp = (Queue(n) for n in ("pe", "act", "dve", "pool", "sp"))
        self.queues = [self.pe, self.act, self.dve, self.pool, self.sp]
        self.counts = {}
        self.nsem = 0

    def sem(self, name):
        self.nsem += 1
        return self.ctx.enter_context(self.nc.semaphore(name))

    def dma(self, queue, sem, out, in_, *waits):
        v = self.counts.get(id(sem), 0) + 16
        self.counts[id(sem)] = v
        queue.ops.append((flat(waits), lambda e: e.dma_start(out, in_), None, sem))
        return DmaToken(sem, v)

    def fence(self):
        return [t for q in (self.pe, self.act, self.dve, self.pool) for t in q.last()
                if isinstance(t, Token)]

    def emit(self, block, ends):
        for q in self.queues:
            q.close()
        used = {id(t) for q in self.queues for w, _, _, _ in q.ops for t in w}
        for q in self.queues:
            q.sem = self.sem("done_" + q.name)
            n = 0
            for _, _, t, _ in q.ops:
                if t is not None:
                    if id(t) in used:
                        n += 1
                        t.value = n

        def body(q):
            def run(eng):
                seen = {}
                for waits, fn, t, dsem in q.ops:
                    need = {}
                    for w in waits:
                        s = w.eng.sem if isinstance(w, Token) else w.sem
                        if w.value > max(seen.get(id(s), 0), need.get(id(s), (None, 0))[1]):
                            need[id(s)] = (s, w.value)
                    for k, (s, v) in need.items():
                        eng.wait_ge(s, v)
                        seen[k] = v
                    ins = fn(eng)
                    if dsem is not None:
                        ins.then_inc(dsem, 16)
                    elif t.value is not None:
                        ins.then_inc(q.sem, 1)
                if q is self.sp:
                    for t in ends:
                        eng.wait_ge(t.sem, t.value)
            return run

        block.tensor(body(self.pe))
        block.scalar(body(self.act))
        block.vector(body(self.dve))
        block.gpsimd(body(self.pool))
        block.sync(body(self.sp))


class Ring:

    def __init__(self, items, free=()):
        self.free = [(i, list(free)) for i in items]

    def take(self):
        return self.free.pop(0)

    def give(self, item, *tokens):
        self.free.append((item, flat(tokens)))


class Banks:

    def __init__(self, n=8):
        self.free = [(i, []) for i in range(n)]

    def take(self):
        return self.free.pop(0)

    def pair(self):
        for i, (b, w) in enumerate(self.free):
            for j, (c, v) in enumerate(self.free):
                if b % 2 == 0 and c == b + 1:
                    for x in sorted((i, j), reverse=True):
                        self.free.pop(x)
                    return b, w + v
        raise RuntimeError("no pair of banks")

    def give(self, b, *tokens):
        self.free.append((b, flat(tokens)))

    def give_pair(self, b, *tokens):
        self.give(b, *tokens)
        self.give(b + 1, *tokens)


def rope_tables(rot, copies, pad):
    n = np.arange(LAT)
    row, col = (n // 64).astype(np.float32), (n % 64).astype(np.float32)
    axis = rot // 2
    inv = (np.float32(10000.0) ** (-np.arange(0, axis, 2, dtype=np.float32) / np.float32(axis))).astype(np.float32)
    parts = []
    for pos in (row, col):
        ang = (pos[:, None] * inv[None, :]).astype(np.float32).T
        parts += [ang, ang]
    ang = np.concatenate(parts, 0)
    c, s = np.cos(ang).astype(np.float32), np.sin(ang).astype(np.float32)
    if pad:
        c = np.concatenate([np.ones((pad, LAT), np.float32), c], 0)
        s = np.concatenate([np.zeros((pad, LAT), np.float32), s], 0)
    return np.tile(c, (copies, 1)), np.tile(s, (copies, 1))


def rope_swap(rot, copies, pad):
    q = rot // 4
    n = (rot + pad) * copies
    m = np.zeros((n, n), np.float32)
    for c in range(copies):
        for half in range(2):
            o = c * (rot + pad) + pad + half * 2 * q
            for i in range(q):
                m[o + q + i, o + i] = -1.0
                m[o + i, o + q + i] = 1.0
    return m


def constants():
    p = np.arange(128)
    k = {}
    k["ident"] = np.eye(128, dtype=np.float32)
    k["ones"] = np.ones((128, 128), np.float32)
    k["mean"] = np.full((128, 128), 1.0 / 1024, np.float32)
    k["head64"] = (p[:, None] // 64 == p[None, :] // 64).astype(np.float32)
    k["swap64"] = rope_swap(64, 2, 0)
    s96 = np.zeros((128, 128), np.float32)
    s96[:96, :96] = rope_swap(32, 1, 64)
    k["swap96"] = s96
    k["causal"] = (p[:, None] <= p[None, :]).astype(np.float32)
    k["cmask"] = ((p[:, None] // 64) == (p[None, :] // 16) % 2).astype(np.float32)
    sel = np.zeros((128, 512), np.float32)
    for h in range(4):
        sel[h, h * 128:(h + 1) * 128] = 1.0
    mats = np.concatenate([k[n] for n in MATS] + [sel], 1)
    c64, s64 = rope_tables(64, 2, 0)
    c96, s96t = rope_tables(32, 1, 64)
    z = np.zeros((32, LAT), np.float32)
    turn = np.stack([c64, s64, np.concatenate([c96, z]), np.concatenate([s96t, z])])
    masks = []
    for h in (64, 32, 16, 8, 4, 2, 1):
        b = p // (2 * h)
        masks.append((b[:, None] == b[None, :]) & ((p % (2 * h)) < h)[:, None] & ((p % (2 * h)) >= h)[None, :])
    masks.append(np.eye(128, dtype=bool))
    masks = np.concatenate(masks, 1).astype(np.float32)
    return {"k_mats": mats, "k_turn": turn, "k_masks": masks}


MATS = ["ident", "ones", "mean", "head64", "swap64", "swap96", "causal", "cmask"]


def build(nc, a, out, parts=("l0", "l1", "mix", "ffn")):
    ctx = ExitStack()
    with ctx:
        P = Program(nc, ctx)
        pe, act, dve, pool, sp = P.queues

        def cp(q, out_, in_, *w):
            return q(lambda e: e.tensor_copy(out_, in_), *w)

        def fill(q, out_, v, *w):
            return q(lambda e: e.memset(out_, v), *w)

        def recip(q, out_, in_, *w):
            return q(lambda e: e.reciprocal(out_, in_), *w)

        def scan(q, out_, d0, d1, first, o0, o1, *w):
            return q(lambda e: e.tensor_tensor_scan(out_, d0, d1, first, o0, o1), *w)

        def cpred(q, out_, mask, data, *w):
            return q(lambda e: e.copy_predicated(out_, mask, data), *w)

        def trp(q, out_, in_, idn, *w):
            return q(lambda e: e.transpose(out_, in_, idn), *w)

        def sb(name, shape, dt=F32):
            return ctx.enter_context(nc.sbuf_tensor(name, shape, dt))

        X = sb("X", [128, 8, TOK])
        H = sb("H", [128, 2, 8, TOK], BF)
        AR = sb("AR", [128, 24576])
        WS = sb("WS", [128, 2, 2048])
        WB = sb("WB", [128, 2, 2, 2048], BF)
        GT = sb("GT", [128, 4, 512])
        EB = sb("EB", [128, 2048])
        KM = sb("KM", [128, 8 * 128])
        MOD = sb("MOD", [128, 2, 48, 2])
        SM = sb("SM", [128, 704])
        STATS = sb("STAT", [128, 1280])
        STAT = [STATS[:, 0:512], STATS[:, 512:1024], STATS[:, 1024:1280]]
        PS = ctx.enter_context(nc.psum_tensor("PS", [128, 8, 512], F32))
        EDR = nc.dram_tensor("e_scratch", (16, 128, 1024), F32, kind="Internal").ap()
        mat = {n: KM[:, i * 128:(i + 1) * 128] for i, n in enumerate(MATS)}
        banks = Banks()

        def ps(b, n=512, rows=slice(0, 128)):
            return PS[rows, b, 0:n]

        def ps2(b, rows=slice(0, 128)):
            return PS[rows, b:b + 2, :].rearrange("p a b -> p (a b)")

        smo, smn = {}, [0]

        def col(name, n, rows=slice(0, 128)):
            if name not in smo:
                smo[name] = smn[0]
                smn[0] += n
                assert smn[0] <= 684
            o = smo[name]
            return SM[rows, o:o + n]

        s_const, s_rows = P.sem("s_const"), P.sem("s_rows")
        ROWS = EB[:, 0:384].rearrange("p (g n) -> p g n", n=128)
        tz = fill(dve, EB[:, 0:384], 0.0)
        tC = P.dma(sp, s_const, KM[:, :], a["k_mats"][:, 0:8 * 128])
        trow = []

        def columns(name, n, *srcs):
            if smn[0] // 128 != (smn[0] + n - 1) // 128:
                smn[0] = -(-smn[0] // 128) * 128
            c = col(name, n)
            g, r = divmod(smo[name], 128)
            for src, r0, c0 in srcs:
                trow.append(P.dma(sp, s_rows, ROWS[r + r0:r + r0 + src.shape[0], g, c0:c0 + src.shape[1]], src, tz))
            return c

        def rows_of(v):
            return v.rearrange("(f p) -> f p", p=128)

        def one(v):
            return v.rearrange("(o p) -> o p", o=1)

        cvec = columns("cvec", 24, (rows_of(a["c"][0]), 0, 0), (rows_of(a["c_ctx"]), 8, 0),
                       (rows_of(a["c_2"][0]), 16, 0)).rearrange("p (v f) -> p f v", v=3)
        ADB = [columns(f"adb{i}", 48, (rows_of(a["b_ada"][i]), 0, 0)) for i in range(2)]
        adb2 = columns("adb2", 48, (rows_of(a["ada_b_2"][0]), 0, 0))
        lng = columns("lng", 32, *[(rows_of(a["ln_g"][i, j]), 16 * i + 8 * j, 0) for i in range(2) for j in range(2)])
        lnb = columns("lnb", 32, *[(rows_of(a["ln_b"][i, j]), 16 * i + 8 * j, 0) for i in range(2) for j in range(2)])
        lng, lnb = (v.rearrange("p (i f) -> p i f", f=8) for v in (lng, lnb))
        qg, kg = (columns(n, 1, (one(a[n][0]), 0, 0), (one(a[n][0]), 0, 64)) for n in ("gqa_q_norm", "gqa_k_norm"))
        mqg = columns("mqg", 3, (rows_of(a["mla_q_norm"][0]), 0, 0))
        mkg = columns("mkg", 2, (rows_of(a["mla_kv_norm"][0]), 0, 0))
        nrm = {n: columns(n, 8, (rows_of(a[n][0]), 0, 0)) for n in ("pre1_w_2", "post1_w_2", "pre2_w_2", "post2_w_2")}
        glab = columns("glab", 2, (rows_of(a["gla_a_b_2"][0]), 0, 0))
        glanw = columns("glanw", 4, (rows_of(a["gla_norm_w_2"][0]), 0, 0))
        cw = columns("cw", 16, *[(rows_of(a["ml_conv_w_2"][0, j]), 4 * j, 0) for j in range(4)])
        cw = cw.rearrange("p (j f) -> p j f", f=4)
        cb = columns("cb", 4, (rows_of(a["ml_conv_b_2"][0]), 0, 0))
        ib = columns("ib", 1, (one(a["ml_i_b_2"][0]), 0, 0), (one(a["ml_f_b_2"][0]), 0, 32))
        glub = columns("glub", 4, (rows_of(a["s5_glu_b_2"][0]), 0, 0))
        bgb = columns("bgb", 24, (rows_of(a["branch_gate_b_2"][0]), 0, 0))
        s5d = columns("s5d", 4, (rows_of(a["s5_d_2"][0]), 0, 0))
        lre = columns("lre", 16, (a["s5_lam_re_2"][0].rearrange("(r g) p -> r (g p)", g=2), 0, 0))
        lim = columns("lim", 16, (a["s5_lam_im_2"][0].rearrange("(r g) p -> r (g p)", g=2), 0, 0))
        assert smn[0] <= 384
        smn[0] = 384
        lst = P.dma(sp, s_rows, EB[0:16, 384:386], a["s5_log_step_2"][0].rearrange("(r g) -> r g", g=2))
        lrow = cp(dve, EB[0:16, 512:640].rearrange("p (g n) -> p g n", n=64), EB[0:16, 384:386].unsqueeze(2).to_broadcast([16, 2, 64]), lst)
        dt = col("dt", 16)
        epsc, onec = col("epsc", 1), col("onec", 1)
        t1 = fill(dve, epsc, EPS)
        t2 = fill(dve, onec, 1.0)
        ident = mat["ident"]
        t = trp(pe, PS[:, 0, 0:128], ROWS[:, 0, :], ident, tC, trow, lst, lrow)
        t = trp(pe, PS[:, 0, 128:256], ROWS[:, 1, :], ident)
        t = trp(pe, PS[:, 0, 256:384], ROWS[:, 2, :], ident)
        t = trp(pe, PS[:, 0, 384:400], EB[0:16, 512:640], ident[0:16, 0:16])
        t = cp(dve, SM[:, 0:400], PS[:, 0, 0:400], t)
        b0, _ = banks.take()
        banks.give(b0, t)
        IDB = sb("IDB", [128, 128], BF)
        tib = cp(dve, IDB[:, :], ident, tC)
        K = [tC, t1, t2, t, tib]

        def mm(out_, l, r, start, stop, *w):
            return pe(lambda e: e.matmul(out_, l, r, start=start, stop=stop), *w)

        def tr(out_, in_, n, *w):
            return trp(pe, out_, in_, mat["ident"][0:n, 0:n], *w)

        def tt(q, out_, i0, i1, op, *w):
            return q(lambda e: e.tensor_tensor(out_, i0, i1, op), *w)

        def ts(q, out_, i0, s1, s2, o0, o1, *w):
            if o1 is None:
                return q(lambda e: e.tensor_scalar(out_, i0, s1, None, o0), *w)
            return q(lambda e: e.tensor_scalar(out_, i0, s1, s2, o0, o1), *w)

        def stt(out_, i0, s, i1, o0, o1, *w):
            return dve(lambda e: e.scalar_tensor_tensor(out=out_, in0=i0, scalar=s, in1=i1, op0=o0, op1=o1), *w)

        def af(out_, in_, f, *w, bias=None, scale=None, accum=None):
            kw = {}
            if bias is not None:
                kw["bias"] = bias
            if scale is not None:
                kw["scale"] = scale
            if accum is not None:
                kw["accum_out"] = accum
            return act(lambda e: e.activation(out_, in_, f, **kw), *w)

        MUL, ADD, SUB, MAX, MIN = ALU.mult, ALU.add, ALU.subtract, ALU.max, ALU.min

        side = []
        ahead = [act.place(), dve.place()]
        apart = []

        def step():
            if ahead[1] is None:
                ahead[1] = dve.place()
            for g in list(side):
                try:
                    next(g)
                except StopIteration:
                    side.remove(g)

        def drain():
            while side:
                step()

        wsem = [P.sem(f"s_w{i}") for i in range(6)]
        stage_at = [WS[:, i, :] for i in range(2)] + [AR[:, 9216 + i * 2048:11264 + i * 2048] for i in range(4)]
        split_at = [WB[:, i, :, :] for i in range(2)]
        split_at += [AR[:, o:o + 2048].bitcast(BF).rearrange("p (h n) -> p h n", h=2) for o in (17408, 19456)]
        wstage = Ring(range(6))
        wsplit = Ring(range(4))

        def weights(srcs, nk, n, whole=False, zero=False):
            slot, w = wstage.take()
            v = stage_at[slot][:, 0:nk * n].rearrange("p (k n) -> p k n", n=n)
            if not isinstance(srcs, list):
                srcs = [(srcs, 0)]
            if zero:
                w = fill(pool, v, 0.0, w)
                ahead[:] = [act.place(), None if apart else dve.place()]
            for src, c0 in srcs:
                t = P.dma(sp, wsem[slot], v[:, :, c0:c0 + src.shape[1]], src.rearrange("(k p) n -> p k n", p=128), w)
            if whole:
                return ("s", slot), v, None, t
            ps_, w = wsplit.take()
            hi, lo = (split_at[ps_][:, i, 0:nk * n] for i in range(2))
            st = stage_at[slot][:, 0:nk * n]
            pa, pd = ahead[0], dve.place() if ahead[1] is None else ahead[1]
            ahead[:] = [act.place(), None if apart else dve.place()]
            th = act(lambda e: e.activation(hi, st, ACT.Copy), t, w, at=pa)
            tl = dve(lambda e: e.tensor_tensor(lo, st, hi, ALU.subtract), th, w, at=pd)
            wstage.give(slot, tl)
            r = lambda x: x.rearrange("p (k n) -> p k n", n=n)
            return ("b", ps_), r(hi), r(lo), [th, tl]

        def release(slot, *t):
            (wstage if slot[0] == "s" else wsplit).give(slot[1], *t)
            if slot[0] == "s":
                ahead[:] = [act.place(), None if apart else dve.place()]

        def mm3(out_, l, r, start, stop, *w):
            mm(out_, l[0], r[0], start, False, *w)
            mm(out_, l[0], r[1], False, False)
            return mm(out_, l[1], r[0], False, stop)

        def split(src, dst, *w, q=None):
            t = af(dst[0], src, ACT.Copy, *w)
            return tt(q or dve, dst[1], src, dst[0], SUB, t)

        def own_slots():
            for r, n in ((wstage, 2), (wsplit, 2)):
                r.free = sorted((x for x in r.free if x[0] < n), key=lambda x: x[0])

        def linear(src, units, nks, rhs, segs, evac, whole=False):
            for c0, nc_, ms in units:
                accs = {}
                k0 = 0
                kt = sum(nks)
                for nk in nks:
                    slot, v, vl, t = weights(src[k0 * 128:(k0 + nk) * 128, c0:c0 + nc_], nk, nc_, whole)
                    for key, off, M in ms:
                        for s in segs:
                            if k0 == 0:
                                accs[key, s] = banks.take()
                            b, bw = accs[key, s]
                            n = SEG[s][1]
                            for k in range(nk):
                                r, rw = rhs(k0 + k, s)
                                c = slice(off, off + M)
                                if whole:
                                    last = mm(ps(b, n, slice(0, M)), v[:, k, c], r, k0 + k == 0, k0 + k == kt - 1, t, bw, rw)
                                else:
                                    last = mm3(ps(b, n, slice(0, M)), (v[:, k, c], vl[:, k, c]), r,
                                               k0 + k == 0, k0 + k == kt - 1, t, bw, rw)
                            if k0 + nk == kt:
                                if (key, off, M) == ms[-1] and s == segs[-1]:
                                    release(slot, last)
                                g = evac(key, s, b, last)
                                if g is not None:
                                    side.append(g)
                                step()
                    if k0 + nk < kt:
                        release(slot, last)
                    k0 += nk

        def tiles(c0, n, per=2):
            return [(c0 + i * 128, min(per, n - i) * 128, [(i + j, j * 128, 128) for j in range(min(per, n - i))])
                    for i in range(0, n, per)]

        sil = col("sil", 24).rearrange("p (f v) -> p f v", v=3)
        sx = col("sx", 24).rearrange("p (f v) -> p f v", v=3)
        t = ts(dve, sx, cvec, -80.0, None, MAX, None, K)
        t = af(sx, sx, ACT.Exp, t, scale=-1.0)
        t = ts(dve, sx, sx, 1.0, None, ADD, None, t)
        t = recip(dve, sx, sx, t)
        tsil = tt(dve, sil, sx, cvec, MUL, t)
        SILB = sb("SILB", [128, 8, 2, 3], BF)
        tsil = split(sil, (SILB[:, :, 0, :], SILB[:, :, 1, :]), tsil)
        modt = {}

        def ada(src, nv, v0, bias, dst, adds, c_from, c_to, key):
            for c in range(c_from, c_to):
                slot, v, vl, t = weights(src[:, c * 256:(c + 1) * 256], 8, 256)
                b, bw = banks.take()
                for j in range(2):
                    cc = slice(128 * j, 128 * j + 128)
                    o4 = PS[:, b, 4 * j:4 * j + 2 * nv].rearrange("p (a v) -> p a v", v=nv)
                    for k in range(8):
                        mm(o4, v[:, k, cc], SILB[:, k, :, v0:v0 + nv], k == 0, False, t, bw, tsil)
                        last = mm(PS[:, b, 4 * j:4 * j + nv], vl[:, k, cc], SILB[:, k, 0, v0:v0 + nv], False, k == 7)
                release(slot, last)
                o = dst[:, 2 * c:2 * c + 2, :]
                pv = PS[:, b, 0:8].rearrange("p (j a v) -> p j a v", j=2, a=4 // nv)
                t = tt(dve, o, pv[:, :, 0, :], bias[:, 2 * c:2 * c + 2].unsqueeze(2).to_broadcast([128, 2, nv]), ADD, last, K)
                t = tt(dve, o, pv[:, :, 1, :], o, ADD, t)
                banks.give(b, t)
                for j in adds:
                    if 4 * j <= c < 4 * j + 4:
                        t = ts(dve, o, o, 1.0, None, ADD, None, t)
                modt[key] = t
                yield

        def ada1(i, c_from, c_to):
            return ada(a["w_ada"][i], 2, 0, ADB[i], MOD[:, i, :, :], (1, 4), c_from, c_to, i)

        def paced(g, n):
            for _ in g:
                for _ in range(n):
                    yield

        def chain(*gs):
            for g in gs:
                yield from g

        def run_all(g):
            for _ in g:
                pass

        MOD2 = col("mod2", 48)

        def ada2():
            return ada(a["ada_w_2"][0], 1, 2, adb2, MOD2.unsqueeze(2), (1, 2, 4, 5), 0, 24, "b2")

        s_x = [P.sem(f"s_x{i}") for i in range(6)]
        xin = AR[:, 0:6 * 1024].rearrange("p (t n) -> p t n", t=6)
        nt = 6 if "l0" in parts or "l1" in parts else 4
        xt = {}
        for t6 in range(nt):
            src = a["x"][0, t6 * 128:(t6 + 1) * 128, :] if t6 < 4 else a["ctx"][0, (t6 - 4) * 128:(t6 - 3) * 128, :]
            td = P.dma(act, s_x[t6], xin[:, t6, :], src)
            for half in range(2):
                b, bw = banks.take()
                for j in range(4):
                    f = half * 4 + j
                    last = tr(PS[:, b, j * 128:(j + 1) * 128], xin[:, t6, f * 128:(f + 1) * 128], 128, td, bw, K)
                dst = X[:, half * 4:half * 4 + 4, t6 * 128:(t6 + 1) * 128]
                src_ = ps(b).rearrange("p (j n) -> p j n", n=128)
                if half:
                    t = cp(dve, dst, src_, last)
                else:
                    t = af(dst, src_, ACT.Copy, last)
                banks.give(b, t)
                for j in range(4):
                    xt.setdefault((half * 4 + j, 0 if t6 < 4 else 1), []).append(t)

        def seg(buf, f, s):
            return buf[:, f, SEG[s][0]:SEG[s][0] + SEG[s][1]]

        ht = {}

        def hseg(f, s):
            o, n = SEG[s]
            return H[:, 0, f, o:o + n], H[:, 1, f, o:o + n]

        def modulate(i, j, segs, tmps, w=()):
            for s in segs:
                for f in range(8):
                    A, B = MOD[:, i, (3 * j + 1) * 8 + f, s:s + 1], MOD[:, i, 3 * j * 8 + f, s:s + 1]
                    x, (h0, h1) = seg(X, f, s), hseg(f, s)
                    y, yw = tmps.take()
                    th = af(h0, x, ACT.Identity, xt[f, s], modt[i], w, scale=A, bias=B)
                    ty = ts(dve, y[:, 0:SEG[s][1]], x, A, B, MUL, ADD, xt[f, s], modt[i], yw)
                    ht[f, s] = [tt(dve, h1, y[:, 0:SEG[s][1]], h0, SUB, ty, th)]
                    tmps.give(y, ht[f, s])
                    if f % 2:
                        xt[f, s] = [ts(pool, x, x, ALPHA, None, MUL, None, ty, th)]
                    else:
                        xt[f, s] = [af(x, x, ACT.Copy, ty, th, scale=ALPHA)]

        def hrhs(k, s):
            return hseg(k, s), ht[k, s]

        means = {}

        def add_mean(f, s):
            if s not in means:
                means[s] = banks.take()
            b, bw = means[s][0:2]
            n = SEG[s][1]
            means[s] = (b, bw, mm(ps(b, n), mat["mean"], seg(X, f, s), f == 0, f == 7, bw, xt[f, s], K))

        def add_gated(i, j):
            due = []

            def evac(f, s, b, t):
                t = stt(seg(X, f, s), ps(b, SEG[s][1]), MOD[:, i, (3 * j + 2) * 8 + f, s:s + 1], seg(X, f, s),
                        MUL, ADD, t, xt[f, s], modt[i])
                banks.give(b, t)
                xt[f, s] = [t]
                due.append((f, s))
                while len(due) > (0 if (f, s) == (7, means_to[-1]) else 2):
                    add_mean(*due.pop(0))

            return evac

        means_to = [1]
        statt = [[], [], []]

        def rstd(b, n, scale, t, o):
            st = STAT[o][:, 0:n]
            t = af(st, ps(b, n), ACT.Ln, t, statt[o], K, bias=epsc, scale=scale)
            banks.give(b, t)
            return af(st, st, ACT.Exp, t, scale=-0.5)

        def layer_norm(ln, segs, tmps, mod=None, w=()):
            square, gain = {}, {}
            for s in segs:
                if mod is not None:
                    i, j = mod
                    sc, sh = MOD[:, i, (3 * j + 1) * 8:(3 * j + 2) * 8, s], MOD[:, i, 3 * j * 8:(3 * j + 1) * 8, s]
                    A, B, AG, AB = (col(f"ln{x}{s}", 8) for x in range(4))
                    t = tt(dve, A, lng[:, ln, :], sc, MUL, K, modt[i], P.fence())
                    t = tt(dve, B, lnb[:, ln, :], sc, MUL)
                    t = tt(dve, B, B, sh, ADD, t)
                    ts(dve, AG, lng[:, ln, :], ALPHA, None, MUL, None)
                    gain[s] = [t, ts(dve, AB, lnb[:, ln, :], ALPHA, None, MUL, None)]
            for s in segs:
                n = SEG[s][1]
                b, _, last = means.pop(s)
                b2, bw2 = banks.take()
                for f in range(8):
                    t = tt(dve, seg(X, f, s), seg(X, f, s), ps(b, n), SUB, last)
                    xt[f, s] = [t]
                    tmp, tw = tmps.take()
                    t2_ = af(tmp[:, 0:n], seg(X, f, s), ACT.Square, t, tw)
                    last2 = mm(ps(b2, n), mat["mean"], tmp[:, 0:n], f == 0, f == 7, bw2, t2_, K)
                    tmps.give(tmp, last2)
                banks.give(b, t)
                square[s] = (b2, last2)
            for s in segs:
                n = SEG[s][1]
                tr_ = rstd(*square[s][0:1], n, 1.0, square[s][1], s)
                for f in range(8):
                    x = seg(X, f, s)
                    t = tt(dve, x, x, STAT[s][:, 0:n], MUL, tr_, xt[f, s])
                    if mod is None:
                        xt[f, s] = [ts(pool if f % 2 else dve, x, x, lng[:, ln, f:f + 1], lnb[:, ln, f:f + 1], MUL, ADD, t, K)]
                        continue
                    A, B, AG, AB = (col(f"ln{y}{s}", 8)[:, f:f + 1] for y in range(4))
                    h0, h1 = hseg(f, s)
                    th = af(h0, x, ACT.Identity, t, gain[s], w, scale=A, bias=B)
                    y, yw = tmps.take()
                    ty = ts(dve, y[:, 0:n], x, A, B, MUL, ADD, t, yw, gain[s])
                    ht[f, s] = [tt(dve, h1, y[:, 0:n], h0, SUB, ty, th)]
                    tmps.give(y, ht[f, s])
                    if f % 2:
                        xt[f, s] = [ts(pool, x, x, AG, AB, MUL, ADD, th, ty)]
                    else:
                        xt[f, s] = [af(x, x, ACT.Identity, th, ty, scale=AG, bias=AB)]
                statt[s] = [t]

        def token_major(src, c0, n, dst, toks, ntt, w):
            slot, v, vl, t = weights(src[:, c0:c0 + n], 8, n)
            for j in range(ntt):
                b, bw = banks.take()
                s = 0 if j < 4 else 1
                for k in range(8):
                    x = (H[:, 0, k, j * 128:(j + 1) * 128], H[:, 1, k, j * 128:(j + 1) * 128])
                    last = mm3(ps(b, n), x, (v[:, k, :], vl[:, k, :]), k == 0, k == 7, bw, t, ht[k, s])
                d = dst(j)
                if isinstance(d, tuple):
                    tk = split(ps(b, n), d, last, w)
                else:
                    tk = af(d, ps(b, n), ACT.Copy, last, w)
                banks.give(b, tk)
                toks.setdefault(j, []).append(tk)
                step()
            release(slot, last)

        def arena(off, *shape):
            n = int(np.prod(shape))
            v = AR[:, off:off + n]
            if len(shape) == 2:
                v = v.rearrange("p (a b) -> p a b", b=shape[1])
            return v

        def arena2(off, *shape):
            n = int(np.prod(shape))
            v = AR[:, off:off + n].bitcast(BF)
            if len(shape) == 2:
                return v.rearrange("p (h a b) -> p h a b", h=2, b=shape[1])
            return v.rearrange("p (h a) -> p h a", h=2)

        def halves(a0, a1):
            return a0.bitcast(BF), a1.bitcast(BF)

        def both(v, *ix):
            return tuple(v[(ix[0], h) + ix[1:]] for h in range(2))

        gtmps = Ring([GT[:, i, :] for i in range(4)])

        def tmp_ring(off, n, fence):
            assert off + n * 512 <= 24576
            return Ring([AR[:, off + i * 512:off + (i + 1) * 512] for i in range(n)], fence)

        def attention(heads, qv, kv, vv, ov, qtiles, keys, Pb, Pc, PTb, rw, before=None):
            nk = keys[1] // 128
            nq = len(qtiles)
            units = [(h, j) for h in heads for j in range(nq)]
            st = {}
            res = {}

            def scores(u):
                h, j = units[u]
                q, qw = qv(h, qtiles[j])
                k, kw = kv(h)
                b, bw = banks.pair()
                S = ps2(b)
                n1 = min(512, keys[1])
                t = mm3(S[:, 0:n1], q, [x[:, keys[0]:keys[0] + n1] for x in k], True, True, bw, qw, kw)
                if keys[1] > 512:
                    t = mm3(S[:, 512:keys[1]], q, [x[:, keys[0] + 512:keys[0] + keys[1]] for x in k], True, True)
                c = rw.take()
                nm, rs = c[0]
                S = S[:, 0:keys[1]]
                t2_ = dve(lambda e: e.tensor_reduce(nm, S, AX.X, MAX, negate=True), t, c[1])
                p, pw = Pb.take()
                Sv = S
                if len(p.shape) == 3:
                    Sv = S.rearrange("p (a b) -> p a b", b=256)
                    pv, like = p, lambda x: x.rearrange("p (a b) -> p a b", b=256)
                else:
                    pv, like = p[:, 0:keys[1]], lambda x: x
                t3 = af(pv, Sv, ACT.Exp, t2_, pw, bias=nm, accum=rs)
                banks.give_pair(b, t3)
                st[u] = (c[0], p, pv, like, t3)

            def normalize(u):
                c, p, pv, like, t3 = st[u]
                t4 = recip(dve, c[1], c[1], t3)
                y, yw = Pc.take()
                t5 = ts(pool, like(y[0][:, 0:keys[1]]), pv, c[1], None, MUL, None, t4, t3, yw)
                st[u] = (c, p, pv, like, y, yw, t5)

            def rest(u):
                c, p, pv, like, y, yw, t5 = st[u]
                t6 = stt(like(y[1][:, 0:keys[1]]), pv, c[1], like(y[0][:, 0:keys[1]]), MUL, SUB, t5, yw)
                rw.give(c, t6)
                Pb.give(p, t6)
                st[u] = (y, t5, t6)

            def turn(u):
                h, j = units[u]
                y, ty, tz = st.pop(u)
                if j == 0:
                    res[h] = PTb.take()
                PT, ptw = res[h]
                b, bw = banks.pair()
                for i in range(2):
                    T = PS[:, b + i, :].bitcast(BF)
                    for k in range(nk):
                        last = trp(pe, T[:, k * 128:(k + 1) * 128], y[i][:, k * 128:(k + 1) * 128], IDB[:, :], ty, tz, bw)
                    dst = PT[:, i, 0:nk, j * 128:(j + 1) * 128]
                    src_ = T[:, 0:nk * 128].rearrange("p (k q) -> p k q", q=128)
                    t = cp(dve, dst, src_, last, ptw) if (i and u % 4) else af(dst, src_, ACT.Copy, last, ptw)
                    banks.give(b + i, t)
                    st[h, "pt"] = st.get((h, "pt"), []) + [t]
                Pc.give(y, last)

            def weigh(u):
                h, j = units[u]
                PT, _ = res[h]
                r0 = 64 * (h % 2)
                if j == 0:
                    res[h, "b"] = banks.take()
                b, bw = res[h, "b"]
                for k in range(j * nk // nq, (j + 1) * nk // nq):
                    v, vw = vv(k, h)
                    last = mm3(ps(b, nq * 128, slice(r0, r0 + 64)), v, [PT[:, i, k, 0:nq * 128] for i in range(2)],
                               k == 0, k == nk - 1, bw, vw, st[h, "pt"])
                if j == nq - 1:
                    PTb.give(PT, last)
                    res[h, "o"] = last

            def store(u):
                h, j = units[u]
                if j == nq - 1:
                    b, _ = res[h, "b"]
                    o, r0, ow = ov(h)
                    t = split(ps(b, nq * 128, slice(r0, r0 + 64)), o, res[h, "o"], ow)
                    banks.give(b, t)
                    res[h, "o"] = t

            apart.append(True)
            for i in range(len(units) + nq + 4):
                if before is not None:
                    before(i)
                for lag, stage in ((1, normalize), (0, scores), (2, rest), (nq + 3, weigh), (3, turn), (nq + 4, store)):
                    if 0 <= i - lag < len(units):
                        stage(i - lag)
                step()
            apart.clear()
            return {h: res[h, "o"] for h in heads}

        red = Ring([(SM[:, 684 + 2 * i:685 + 2 * i], SM[:, 685 + 2 * i:686 + 2 * i]) for i in range(8)])
        s_turn = P.sem("s_turn")

        S5 = {}

        def s5_tables():
            pw = EB[:, 1536:2048].rearrange("p (n v) -> p n v", v=16)
            nx = [0]

            def new():
                nx[0] += 1
                return pw[:, nx[0] - 1, :]

            cs = [(new(), new()) for _ in range(9)]
            mag, zre, zim = col("mag", 16), col("zre", 16), col("zim", 16)
            t = [None]

            todo = []

            def o(fn):
                todo.append(fn)

            def s_(out_, i0, s1, s2, o0, o1=None):
                if o1 is None:
                    o(lambda e: e.tensor_scalar(out_, i0, s1, None, o0))
                else:
                    o(lambda e: e.tensor_scalar(out_, i0, s1, s2, o0, o1))

            def v_(out_, i0, i1, op):
                o(lambda e: e.tensor_tensor(out_, i0, i1, op))

            def f_(out_, i0, s, i1, o0, o1):
                o(lambda e: e.scalar_tensor_tensor(out=out_, in0=i0, scalar=s, in1=i1, op0=o0, op1=o1))

            def copy(out_, i0):
                o(lambda e: e.tensor_copy(out_, i0))

            def series(out_, z, cs_):
                s_(out_, z, cs_[-1], 1.0, MUL, ADD)
                for c in cs_[-2::-1]:
                    v_(out_, out_, z, MUL)
                    s_(out_, out_, c, 1.0, MUL, ADD)

            A, B, C, E_, F_, G_, I_ = (new() for _ in range(7))
            t[0] = ts(dve, A, dt, -87.0, 87.0, MAX, MIN, K, P.fence())
            s_(B, A, 1.4426950408889634, None, MUL)
            Ii = I_.bitcast(I32)
            copy(Ii, B)
            copy(B, Ii)
            f_(A, B, -0.693359375, A, MUL, ADD)
            f_(A, B, 2.12194440e-4, A, MUL, ADD)
            series(C, A, [1.0, 1 / 2, 1 / 3, 1 / 4, 1 / 5, 1 / 6, 1 / 7])
            s_(B, B, 127.0, 8388608.0, ADD, MUL)
            copy(Ii, B)
            v_(A, C, I_, MUL)
            s_(B, lre, -1e-4, None, MIN)
            v_(C, B, A, MUL)
            s_(C, C, -80.0, 1.0 / 256, MAX, MUL)
            series(E_, C, [1 / 2, 1 / 3, 1 / 4, 1 / 5, 1 / 6, 1 / 7])
            v_(E_, E_, C, MUL)
            for _ in range(8):
                s_(C, E_, 2.0, None, ADD)
                v_(E_, E_, C, MUL)
            s_(mag, E_, 1.0, None, ADD)
            v_(A, A, lim, MUL)
            s_(C, A, 0.15915494309189535, None, MUL)
            copy(Ii, C)
            copy(C, Ii)
            f_(A, C, -6.28125, A, MUL, ADD)
            f_(A, C, -0.0019350051879882812, A, MUL, ADD)
            f_(A, C, -3.0199160501e-07, A, MUL, ADD)
            s_(A, A, 0.5, None, MUL)
            v_(C, A, A, MUL)
            series(F_, C, [-1 / 6, -1 / 20, -1 / 42, -1 / 72, -1 / 110, -1 / 156])
            v_(F_, F_, A, MUL)
            series(G_, C, [-1 / 2, -1 / 12, -1 / 30, -1 / 56, -1 / 90, -1 / 132, -1 / 182])
            v_(C, F_, F_, MUL)
            s_(C, C, -2.0, None, MUL)
            s_(cs[0][0], C, 1.0, None, ADD)
            f_(cs[0][1], F_, 2.0, G_, MUL, MUL)
            f_(A, E_, 1.0, C, ADD, MUL)
            v_(A, A, E_, ADD)
            v_(C, mag, cs[0][1], MUL)
            v_(F_, B, B, MUL)
            v_(G_, lim, lim, MUL)
            v_(F_, F_, G_, ADD)
            o(lambda e: e.reciprocal(F_, F_))
            v_(G_, A, B, MUL)
            v_(I_, C, lim, MUL)
            v_(G_, G_, I_, ADD)
            v_(zre, G_, F_, MUL)
            v_(G_, C, B, MUL)
            v_(I_, A, lim, MUL)
            v_(G_, G_, I_, SUB)
            v_(zim, G_, F_, MUL)
            for j in range(8):
                c, s = cs[j]
                v_(A, s, s, MUL)
                s_(cs[j + 1][0], A, -2.0, 1.0, MUL, ADD)
                f_(cs[j + 1][1], s, 2.0, c, MUL, MUL)
            for i in range(0, len(todo), 10):
                for fn in todo[i:i + 10]:
                    t[0] = dve(fn, t[0])
                yield
            S5["p"] = t[0]
            E_ = EB[:, 0:1024].rearrange("p (a n) -> p a n", n=512)
            T_ = EB[:, 1024:1536].rearrange("p (a n) -> p a n", n=256)
            sd = P.sem("s_tab")
            S5["d"] = []
            td = S5["p"]
            for r in range(16):
                tc_ = fill(pool, E_[:, 0, 0:1], 1.0, td)
                tq = fill(pool, E_[:, 1, 0:1], 0.0, td)
                for j in range(9):
                    n = 1 << j
                    c, s = cs[j][0][:, r:r + 1], cs[j][1][:, r:r + 1]
                    t1_ = ts(pool, T_[:, :, 0:n], E_[:, :, 0:n], s, None, MUL, None, tc_, tq, S5["p"])
                    t2_ = ts(pool, E_[:, :, n:2 * n], E_[:, :, 0:n], c, None, MUL, None)
                    tc_ = tt(pool, E_[:, 0, n:2 * n], E_[:, 0, n:2 * n], T_[:, 1, 0:n], SUB, t1_, t2_)
                    tq = tt(pool, E_[:, 1, n:2 * n], E_[:, 1, n:2 * n], T_[:, 0, 0:n], ADD, t1_, t2_)
                td = P.dma(pool, sd, EDR[r], E_.rearrange("p a n -> p (a n)"), tc_, tq)
                S5["d"].append(td)
                for _ in range(3):
                    yield

        if "l0" in parts:
            TURN = EB[:, 0:1024].rearrange("p (a n) -> p a n", n=512)
            tturn = [P.dma(sp, s_turn, TURN, a["k_turn"][0:2].rearrange("a p n -> p a n"), K)]
            run_all(ada1(0, 0, 8))
            own_slots()
            modulate(0, 0, (0, 1), tmp_ring(6144, 6, []))
            fence = P.fence()
            q_ = arena2(0, 8, TOK)
            k_ = arena2(6144, 8, TOK)
            V_ = arena2(12288, 6, 256)
            Pbuf = [arena(13824 + i * 768, 768) for i in range(3)]
            Pcb = [halves(arena(16128 + i * 384, 384), arena(16512 + i * 384, 384)) for i in (0, 2, 4)]
            PTbuf = [arena2(18432 + i * 3072, 6, 512) for i in range(2)]
            tmps = tmp_ring(17664, 12, fence)
            tkz = fill(pool, AR[:, 6144:12288], 0.0, fence)
            qt_, kt_, vt_ = {}, {}, {}

            def norm_rope(dsts, s, b, t, gain, scale, store):
                n = SEG[s][1]
                (rawb, w1), (sqb, w2) = tmps.take(), tmps.take()
                raw, sq = rawb[:, 0:n], sqb[:, 0:n]
                t2_ = af(sq, ps(b, n), ACT.Square, t, w2)
                t1_ = ts(dve, raw, ps(b, n), gain, scale, MUL, MUL, t, w1, t2_, K)
                banks.give(b, t1_)
                yield
                b, bw = banks.take()
                t = mm(ps(b, n), mat["head64"], sq, True, True, bw, t2_, K)
                t = af(sq, ps(b, n), ACT.Ln, t, bias=epsc, scale=1.0 / 64)
                banks.give(b, t)
                t = af(sq, sq, ACT.Exp, t, scale=-0.5)
                t = tt(dve, raw, raw, sq, MUL, t1_, t)
                if s == 0:
                    yield
                    b, bw = banks.take()
                    tp = mm(ps(b, n), mat["swap64"], raw, True, True, bw, t, K)
                    tc = tt(pool, raw, raw, TURN[:, 0, :], MUL, t, tturn, tp)
                    t2_ = tt(dve, sq, ps(b, n), TURN[:, 1, :], MUL, tp, tturn, t)
                    banks.give(b, t2_)
                    t = tt(dve, raw, raw, sq, ADD, tc, t2_)
                toks = [split(raw[r], dst, t, fence, tkz, q=pool if len(dsts) == 1 else dve) for dst, r in dsts]
                tmps.give(rawb, toks)
                tmps.give(sqb, toks)
                store(toks)

            def evac_qkv(m, s, b, t):
                if m < 8:
                    r = slice(0, 128)
                    o0, n = SEG[s]
                    return norm_rope([((q_[:, 0, m, o0:o0 + n], q_[:, 1, m, o0:o0 + n]), r)], s, b, t, qg, 0.125,
                                     lambda tk: qt_.setdefault((m, s), []).extend(tk))
                m -= 8
                lo, hi = slice(0, 64), slice(64, 128)
                o0, n = SEG[s]

                def kz(i, r):
                    return k_[r, 0, i, o0:o0 + n], k_[r, 1, i, o0:o0 + n]

                d = [(kz(4 * m, lo), lo), (kz(4 * m + 3, hi), hi)]

                def store(tk):
                    t1_ = [cp(dve, x, y, tk) for x, y in zip(kz(4 * m + 1, hi), kz(4 * m, lo))]
                    t2_ = [cp(dve, x, y, tk) for x, y in zip(kz(4 * m + 2, lo), kz(4 * m + 3, hi))]
                    for i, t_ in enumerate((tk, t1_, t2_, tk)):
                        kt_[4 * m + i, s] = t_
                return norm_rope(d, s, b, t, kg, 1.0, store)

            linear(a["gqa_w_qkv"][0], tiles(0, 10), [8], hrhs, (0, 1), evac_qkv)

            token_major(a["gqa_w_qkv"][0], 1280, 256, lambda j: (V_[:, 0, j, :], V_[:, 1, j, :]), vt_, 6, fence)
            drain()
            hfence = pe.last()
            fence = P.fence()
            Pb, Pc, PTb = Ring(Pbuf, fence), Ring(Pcb, fence), Ring(PTbuf, fence)
            side.append(chain(paced(ada1(0, 8, 24), 3), paced(ada1(1, 0, 24), 4)))

            def q_view(h, j):
                return [q_[:, i, h // 2, j * 128:(j + 1) * 128] for i in range(2)], qt_[h // 2, 0 if j < 4 else 1]

            def k_view(h):
                i = 2 * (h // 4) + h % 2
                return [k_[:, 0, i, :], k_[:, 1, i, :]], kt_[i, 0] + kt_[i, 1]

            def v_view(base):
                return lambda k, h: ([V_[:, i, base + k, (h // 4) * 64:(h // 4) * 64 + 64] for i in range(2)], vt_[base + k])

            def o_view(s):
                def o(h):
                    r0 = 64 * (h % 2)
                    return [H[r0:r0 + 64, i, h // 2, SEG[s][0]:SEG[s][0] + SEG[s][1]] for i in range(2)], r0, hfence
                return o

            o1 = attention(range(16), q_view, k_view, v_view(0), o_view(0), [0, 1, 2, 3], (0, 768), Pb, Pc, PTb, red)
            o2 = attention(range(16), q_view, k_view, v_view(4), o_view(1), [4, 5], (512, 256), Pb, Pc, PTb, red)
            for f in range(8):
                ht[f, 0] = [o1[2 * f], o1[2 * f + 1]]
                ht[f, 1] = [o2[2 * f], o2[2 * f + 1]]
            linear(a["gqa_w_o"][0], tiles(0, 8), [8], hrhs, (0, 1), add_gated(0, 0))

        def mlp(i, segs, beside=()):
            tm = tmp_ring(0, 8, P.fence())
            layer_norm(2 * i, segs, tm, (i, 1), pe.last())
            fence = P.fence()
            hid = arena2(0, 32, TOK)
            hidt = {}

            def evac(m, s, b, t):
                o0, n = SEG[s]
                (x, w1), (y, w2) = gtmps.take(), gtmps.take()
                t = af(x[:, 0:n], ps(b, n), ACT.Relu, t, w1)
                banks.give(b, t)
                h0, h1 = (hid[:, j, m, o0:o0 + n] for j in range(2))
                t1_ = af(h0, x[:, 0:n], ACT.Square, t, fence)
                t2_ = tt(dve, y[:, 0:n], x[:, 0:n], x[:, 0:n], MUL, t, w2)
                t = tt(dve, h1, y[:, 0:n], h0, SUB, t1_, t2_)
                gtmps.give(x, t1_, t2_)
                gtmps.give(y, t)
                hidt[m, s] = [t]

            side.extend(beside)
            linear(a["mlp_w1"][i], tiles(0, 32), [8], hrhs, segs, evac)
            linear(a["mlp_w2"][i], tiles(0, 8), [8, 8, 8, 8], lambda k, s: ([hid[:, j, k, SEG[s][0]:SEG[s][0] + SEG[s][1]] for j in range(2)], hidt[k, s]), segs,
                   add_gated(i, 1))
            tm = tmp_ring(0, 8, P.fence())
            if i == 0 and "l1" in parts:
                drain()
                layer_norm(1, segs, tm, (1, 0), pe.last())
            else:
                layer_norm(2 * i + 1, segs, tm)

        if "l0" in parts:
            mlp(0, (0, 1), [s5_tables()])

        if "l1" in parts:
            own_slots()
            drain()
            if 1 not in modt:
                run_all(ada1(1, 0, 24))
            if "l0" not in parts:
                modulate(1, 0, (0, 1), tmp_ring(6144, 8, P.fence()), pe.last())
            means_to.append(0)
            fence = P.fence()
            cqb, ckvb, kpe = arena2(0, 3, 512), arena2(1536, 2, TOK), arena2(3072, 768)
            grp = [(arena2(3840 + g * 6656, 4, TOK), arena2(6912 + g * 6656, 4, 512), arena2(8960 + g * 6656, 6, 256))
                   for g in range(2)]
            Pbuf = [X[:, 0:3, 512:768], X[:, 3:6, 512:768], EB[:, 1024:1792]]
            Pcb = [halves(arena(17152, 384), arena(17536, 384)), halves(STATS[:, 0:384], STATS[:, 384:768]),
                   halves(STATS[:, 768:1152], arena(17920, 384))]
            PTbuf = [arena2(18432 + i * 3072, 6, 512) for i in range(2)]
            cq, ckv = arena(20992, 3, 512), arena(22528, 2, TOK)
            tmps = gtmps
            TURN = EB[:, 0:1024].rearrange("p (a n) -> p a n", n=512)
            tturn = [P.dma(pool, P.sem("s_turn2"), TURN, a["k_turn"][2:4].rearrange("a p n -> p a n"), fence)]
            ct = {}
            W_IN = a["mla_w_in"][0]

            def evac_c(m, s, b, t):
                if m < 3 and s == 1:
                    raise AssertionError
                dst = cq[:, m, :] if m < 3 else seg(ckv, m - 3, s)
                t = af(dst, ps(b, SEG[s][1]), ACT.Copy, t, fence)
                banks.give(b, t)
                ct[m, s] = [t]

            linear(W_IN, tiles(0, 3), [8], hrhs, (0,), evac_c)
            linear(W_IN, [(384, 256, [(3, 0, 128), (4, 128, 128)])], [8], hrhs, (0, 1), evac_c)
            r96, rp = slice(0, 96), slice(64, 96)
            kpt = {}

            def rope96(b, n, t, dst, lat, scale, store, only_pe, w=()):
                x, w1 = tmps.take()
                if not lat:
                    t = split(ps(b, n, rp), [x_[rp, :] for x_ in dst], t, fence)
                    banks.give(b, t)
                    tmps.give(x, w1)
                    store([t])
                    return
                t = af(x[r96, :], ps(b, n, r96), ACT.Copy, t, w1, scale=scale)
                banks.give(b, t)
                b, bw = banks.take()
                tp = mm(ps(b, n, r96), mat["swap96"][r96, 0:96], x[r96, :], True, True, bw, t, K)
                y, w2 = tmps.take()
                ty = tt(dve, y[r96, :], ps(b, n, r96), TURN[r96, 1, :], MUL, tp, w2, tturn)
                banks.give(b, ty)
                tx = tt(pool, x[r96, :], x[r96, :], TURN[r96, 0, :], MUL, tp, tturn)
                rows = rp if only_pe else r96
                t = tt(dve, x[rows, :], x[rows, :], y[rows, :], ADD, tx, ty)
                t = split(x[rows, :], [x_[rows, :] for x_ in dst], t, fence, w)
                tmps.give(x, t)
                tmps.give(y, t)
                store([t])

            def evac_kpe(m, s, b, t):
                o0, n = SEG[s]
                rope96(b, n, t, [kpe[:, i, o0:o0 + n] for i in range(2)], s == 0, 1.0, lambda tk: kpt.__setitem__(s, tk), True)

            linear(W_IN, [(576, 96, [(0, 0, 96)])], [8], hrhs, (0, 1), evac_kpe)
            hfence = pe.last()

            def rms(src, n_t, s, gains, scale, toks, o, dst):
                n = SEG[s][1]
                b, bw = banks.take()
                for f in range(n_t):
                    tmp, tw = tmps.take()
                    t = af(tmp[:, 0:n], src(f), ACT.Square, toks[f], tw)
                    last = mm(ps(b, n), mat["ones"], tmp[:, 0:n], f == 0, f == n_t - 1, bw, t, K)
                    tmps.give(tmp, last)
                tr_ = rstd(b, n, scale, last, o)
                res = []
                for f in range(n_t):
                    t = stt(src(f), src(f), gains[:, f:f + 1], STAT[o][:, 0:n], MUL, MUL, tr_, toks[f])
                    res.append([split(src(f), dst(f), t, fence)])
                statt[o] = res[-1]
                return res

            r_ = rms(lambda f: cq[:, f, :], 3, 0, mqg, 1.0 / 384, [ct[f, 0] for f in range(3)], 0,
                     lambda f: both(cqb, slice(None), f))
            for f in range(3):
                ct[f, 0] = r_[f]
            for s in (0, 1):
                r_ = rms(lambda f: seg(ckv, f, s), 2, s, mkg, 1.0 / 256, [ct[3 + f, s] for f in range(2)], 1 + s,
                         lambda f: [ckvb[:, i, f, SEG[s][0]:SEG[s][0] + SEG[s][1]] for i in range(2)])
                for f in range(2):
                    ct[3 + f, s] = r_[f]
            pfence = P.fence()
            Pb, Pc, PTb = Ring(Pbuf, pfence), Ring(Pcb, pfence), Ring(PTbuf, pfence)
            side.append(paced(ada2(), 4))
            qt_, kt_, vt_ = {}, {}, {}

            def prepare(g, w):
                kT, qT, Vg = grp[g % 2]

                def evac_q(m, b, t):
                    rope96(b, 512, t, both(qT, slice(None), m), True, 96.0 ** -0.5,
                           lambda tk: qt_.__setitem__(4 * g + m, tk), False, w)

                slot, v, vl, t = weights(a["mla_w_uq"][0][:, g * 384:(g + 1) * 384], 3, 384)
                for m in range(4):
                    b, bw = banks.take()
                    for k in range(3):
                        cc = slice(m * 96, m * 96 + 96)
                        last = mm3(ps(b, 512, r96), (v[:, k, cc], vl[:, k, cc]), both(cqb, slice(None), k),
                                   k == 0, k == 2, bw, t, ct[k, 0])
                    if m == 3:
                        release(slot, last)
                    evac_q(m, b, last)
                    yield
                slot, v, vl, t = weights(a["mla_w_ukv"][0][:, g * 512:(g + 1) * 512], 2, 512)
                for m in range(4):
                    for s in (0, 1):
                        n = SEG[s][1]
                        b, bw = banks.take()
                        for k in range(2):
                            cc, sg = slice(m * 128, m * 128 + 64), slice(SEG[s][0], SEG[s][0] + n)
                            last = mm3(ps(b, n, slice(0, 64)), (v[:, k, cc], vl[:, k, cc]),
                                       (ckvb[:, 0, k, sg], ckvb[:, 1, k, sg]), k == 0, k == 1, bw, t, ct[3 + k, s])
                        tk = split(ps(b, n, slice(0, 64)), [kT[0:64, i, m, sg] for i in range(2)], last, w)
                        banks.give(b, tk)
                        kt_.setdefault(4 * g + m, []).append(tk)
                    tk = cp(dve, kT[rp, :, m, :], kpe[rp, :, :], kpt[0], kpt[1], w)
                    kt_[4 * g + m].append(tk)
                    yield
                for j in range(6):
                    b, bw = banks.take()
                    for k in range(2):
                        r = [x[:, k, :].rearrange("p (m c) -> p m c", c=128)[:, :, 64:128] for x in (v, vl)]
                        last = mm3(ps(b, 256).rearrange("p (m c) -> p m c", c=64),
                                   [ckvb[:, i, k, j * 128:(j + 1) * 128] for i in range(2)], r,
                                   k == 0, k == 1, bw, t, ct[3 + k, 0 if j < 4 else 1])
                    if j == 5:
                        release(slot, last)
                    tk = split(ps(b, 256), both(Vg, slice(None), j), last, w)
                    banks.give(b, tk)
                    vt_[g, j] = [tk]
                    yield

            run_all(prepare(0, fence))
            coming = []

            def before(i):
                g, n = divmod(i, 16)
                if n == 8 and g < 3:
                    coming.append(prepare(g + 1, [fence, pe.last()]))
                if coming:
                    for _ in range(2):
                        next(coming[0], None)
                    if n == 15:
                        run_all(coming.pop())

            def o_view(h):
                r0 = 64 * (h % 2)
                return [H[r0:r0 + 64, i, h // 2, 0:512] for i in range(2)], r0, hfence

            oall = attention(range(16), lambda h, j: ([grp[h // 4 % 2][1][r96, i, h % 4, j * 128:(j + 1) * 128]
                                                       for i in range(2)], qt_[h]),
                             lambda h: (both(grp[h // 4 % 2][0], r96, h % 4), kt_[h]),
                             lambda k, h: ([grp[h // 4 % 2][2][:, i, k, (h % 4) * 64:(h % 4) * 64 + 64]
                                            for i in range(2)], vt_[h // 4, k]),
                             o_view, [0, 1, 2, 3], (0, 768), Pb, Pc, PTb, red, before)
            for f in range(8):
                ht[f, 0] = [oall[2 * f], oall[2 * f + 1]]
            statt[:] = [P.fence() for _ in range(3)]
            linear(a["mla_w_o"][0], tiles(0, 8), [8], hrhs, (0,), add_gated(1, 0))
            mlp(1, (0,))

        drain()
        if "mix" in parts and not S5:
            for _ in s5_tables():
                pass
        if "mix" in parts or "ffn" in parts:
            own_slots()
            if "b2" not in modt:
                run_all(ada2())

        def rms_mod(w, j, tmps, hw):
            G = col("G", 8)
            tg = tt(dve, G, w, MOD2[:, (3 * j + 1) * 8:(3 * j + 2) * 8], MUL, modt["b2"], K, dve.last())
            b, bw = banks.take()
            for f in range(8):
                tmp, tw = tmps.take()
                t = af(tmp, seg(X, f, 0), ACT.Square, xt[f, 0], tw)
                last = mm(ps(b), mat["ones"], tmp, f == 0, f == 7, bw, t, K)
                tmps.give(tmp, last)
            tr_ = rstd(b, 512, 1.0 / 1024, last, 0)
            for f in range(8):
                x, xw = tmps.take()
                t = stt(x, seg(X, f, 0), G[:, f:f + 1], STAT[0], MUL, MUL, tr_, tg, xw)
                sh, (h0, h1) = MOD2[:, 3 * j * 8 + f:3 * j * 8 + f + 1], hseg(f, 0)
                th = af(h0, x, ACT.Identity, t, modt["b2"], hw, bias=sh)
                ht[f, 0] = [stt(h1, x, sh, h0, ADD, SUB, th)]
                tmps.give(x, ht[f, 0])
            statt[0] = [t]

        def add_rms(Y, yt, w, j, tmps):
            G = col("G2", 8)
            tg = tt(dve, G, w, MOD2[:, (3 * j + 2) * 8:(3 * j + 3) * 8], MUL, modt["b2"], K, dve.last())
            b, bw = banks.take()
            for f in range(8):
                tmp, tw = tmps.take()
                t = af(tmp, Y[:, f, :], ACT.Square, yt[f], tw)
                last = mm(ps(b), mat["ones"], tmp, f == 0, f == 7, bw, t, K)
                tmps.give(tmp, last)
            tr_ = rstd(b, 512, 1.0 / 1024, last, 1)
            for f in range(8):
                t = stt(Y[:, f, :], Y[:, f, :], G[:, f:f + 1], STAT[1], MUL, MUL, tr_, tg)
                xt[f, 0] = [tt(pool if f % 2 else dve, seg(X, f, 0), seg(X, f, 0), Y[:, f, :], ADD, t, xt[f, 0])]
            statt[1] = [t]

        if "mix" in parts:
            HP = [H[:, i // 8, i % 8, 512:768].bitcast(F32) for i in range(16)]
            XX = [X[:, f, 512:768] for f in range(8)]

            def blk(fs, buf, i):
                return buf[fs[i // 2]][:, 128 * (i % 2):128 * (i % 2) + 128]

            fence = P.fence()
            gqk, gv = arena(0, 4, 512), arena(2048, 4, 512)
            mqk, mv = arena(4096, 4, 516), arena(6160, 4, 512)
            su = arena(8208, 4, 512)
            gr, mo = arena(10256, 4, 512), arena(12304, 4, 512)
            SO = arena(10256, 4, 768)
            cum, EX = arena(14352, 1024), arena(15376, 1024)
            QKL = Ring([arena(16400, 1024)], fence)
            SD = arena(18448, 4, 512)
            tmps = tmp_ring(20496, 3, fence)
            stm = tmp_ring(22032, 4, fence)
            MSK = AR[:, 24080:24336].bitcast(I8).rearrange("p (l n) -> p l n", n=128)
            s_mx = P.sem("s_mx")
            t = P.dma(pool, P.sem("s_mask"), arena(17424, 1024), a["k_masks"], fence)
            tm = [cp(dve, MSK, arena(17424, 1024).rearrange("p (l n) -> p l n", n=128), t)]
            QKL.give(arena(17424, 1024), tm[0])
            for j in range(2):
                tm.append(P.dma(pool, s_mx, XX[j][0:4, :], a["k_mats"][0:4, 1024 + 256 * j:1280 + 256 * j], fence))
            A2 = XX[3][0:16, :]
            tm.append(P.dma(pool, s_mx, A2, a["gla_a2_2"][0], fence))

            def sel(h):
                return XX[h // 2][0:4, 128 * (h % 2):128 * (h % 2) + 128]

            rms_mod(nrm["pre1_w_2"], 0, tmps, pe.last())
            WI = a["w_in_2"][0]
            tok = {}

            def evac_to(buf, base, name, scale=None, off=0):
                def evac(m, s, b, t):
                    t = af(buf[:, m - base, off:off + 512], ps(b), ACT.Copy, t, fence, scale=scale)
                    banks.give(b, t)
                    tok[name, m - base] = [t]
                return evac

            s_b = P.sem("s_b")

            def s5():
                w0 = stm.take()
                w1 = stm.take()
                w2 = stm.take()
                (x0, f0), (x1, f1), (x2, f2) = w0, w1, w2
                bre, bim = x0[:, 0:256], x0[:, 256:512]
                with_ = [f0, f1, f2]
                tb = [P.dma(pool, s_b, bre.rearrange("p (r c) -> p r c", c=16),
                            a["s5_b_re_2"][0].rearrange("(r g) p c -> (g p) r c", g=2), with_),
                      P.dma(pool, s_b, bim.rearrange("p (r c) -> p r c", c=16),
                            a["s5_b_im_2"][0].rearrange("(r g) p c -> (g p) r c", g=2), with_)]
                BRE, BIM, BTR, BTI = (HP[4 * i:4 * i + 4] for i in range(4))
                CTR, CTI = [4, 5], [6, 7]
                tz = [fill(dve, x, 0.0, fence) for x in HP[0:8]]

                def bc(v):
                    return v.unsqueeze(2).to_broadcast([128, 16, 16])

                v3 = lambda x: x.rearrange("p (r c) -> p r c", c=16)
                v4 = lambda x: x.rearrange("p (a r c) -> p a r c", a=4, c=16)
                zr, zi = col("zre", 16), col("zim", 16)
                m = [x1[:, 0:256], x1[:, 256:512], x2[:, 0:256], x2[:, 256:512]]
                q = [tt(dve, v3(m[0]), v3(bre), bc(zr), MUL, tb, S5["p"]),
                     tt(dve, v3(m[1]), v3(bim), bc(zi), MUL, tb),
                     tt(dve, v3(m[2]), v3(bim), bc(zr), MUL, tb),
                     tt(dve, v3(m[3]), v3(bre), bc(zi), MUL, tb)]
                tb2 = []
                for g in range(2):
                    r = slice(64 * g, 64 * g + 64)
                    for fs, p0, p1, op in ((BRE, 0, 1, SUB), (BIM, 2, 3, ADD)):
                        for i in range(4):
                            d = fs[i][r, :].rearrange("p (r c) -> p r c", c=32)[:, :, 16 * g:16 * g + 16]
                            tb2.append(tt(dve, d, v4(m[p0])[r, i], v4(m[p1])[r, i], op, q, tz))
                stm.give(x0, tb2)
                stm.give(x1, tb2)
                stm.give(x2, tb2)
                yield
                tbt = []
                for src, dst in ((BRE, BTR), (BIM, BTI)):
                    b, bw = banks.take()
                    for i in range(4):
                        last = tr(PS[:, b, i * 128:(i + 1) * 128], src[i], 128, tb2, bw)
                    for i in range(4):
                        t = cp(dve, dst[i], PS[:, b, i * 128:(i + 1) * 128], last, fence)
                    tbt.append(t)
                    banks.give(b, t)
                    yield
                tct = []
                for name, dst, sign in (("s5_c_re_2", CTR, 1.0), ("s5_c_im_2", CTI, -1.0)):
                    x, w = stm.take()
                    xv = x.rearrange("p (i n) -> p i n", n=128)
                    src = a[name][0].rearrange("(i g) c p -> (g c) i p", g=8)
                    s_c = P.sem("s_" + name)
                    tcl = [P.dma(pool, s_c, xv[:, :, 64 * g:64 * g + 64], src, w) for g in range(2)]
                    yield
                    b, bw = banks.take()
                    for i in range(4):
                        last = tr(PS[:, b, i * 128:(i + 1) * 128], xv[:, i, :], 128, tcl, bw)
                    for i in range(4):
                        t = stt(blk(dst, XX, i), PS[:, b, i * 128:(i + 1) * 128], sign, mat["cmask"], MUL, MUL, last, fence)
                    stm.give(x, last)
                    banks.give(b, t)
                    tct.append(t)
                    yield
                s_e = [P.sem("s_e0"), P.sem("s_e1")]
                ering = Ring([0, 1], fence)
                mag = col("mag", 16)
                loads = []

                def load(r):
                    e_, ew = ering.take()
                    EV = EB[:, e_ * 1024:(e_ + 1) * 1024]
                    loads.append((e_, EV, P.dma(pool, s_e[e_], EV, EDR[r], ew, S5["d"][r])))

                load(0)
                for i in range(4):
                    yb, ybw = banks.take()
                    for qd in range(4):
                        r = 4 * i + qd
                        e_, EV, te = loads.pop(0)
                        if r < 15:
                            load(r + 1)
                        co, si = EV[:, 0:512], EV[:, 512:1024]
                        rows = slice(32 * qd, 32 * qd + 32)
                        b0, bw0 = banks.take()
                        b1, bw1 = banks.take()
                        l0 = mm(ps(b0), BTR[i][rows, :], su[rows, i, :], True, True, bw0, tbt, tok["su", i])
                        l1 = mm(ps(b1), BTI[i][rows, :], su[rows, i, :], True, True, bw1)
                        ms = [stm.take() for _ in range(4)]
                        (m1, v1), (m2, v2), (m3, v3_), (m4, v4_) = ms
                        t1_ = tt(dve, m1, ps(b0), co, MUL, l0, te, v1)
                        t4_ = tt(dve, m4, ps(b0), si, MUL, v4_)
                        banks.give(b0, t4_)
                        t2_ = tt(dve, m2, ps(b1), si, MUL, l1, v2)
                        t3_ = tt(dve, m3, ps(b1), co, MUL, v3_)
                        banks.give(b1, t3_)
                        ta = tt(pool, m1, m1, m2, ADD, t1_, t2_)
                        tb_ = tt(pool, m3, m3, m4, SUB, t3_, t4_)
                        yield
                        mg = mag[:, r:r + 1].to_broadcast([128, 512])
                        t2_ = scan(dve, m2, mg, m1, 0.0, MUL, ADD, ta)
                        t4_ = scan(dve, m4, mg, m3, 0.0, MUL, ADD, tb_)
                        t1_ = tt(dve, m1, m2, co, MUL, t2_)
                        t3_ = tt(pool, m3, m4, si, MUL, t4_)
                        tx = tt(pool, m1, m1, m3, SUB, t1_, t3_)
                        t4_ = t3_
                        t3_ = tt(pool, m3, m2, si, MUL, tx)
                        yield
                        t4_ = tt(dve, m4, m4, co, MUL, t4_)
                        ty = tt(pool, m3, m3, m4, ADD, t3_, t4_)
                        ering.give(e_, ty)
                        yield
                        last = mm(PS[rows, yb, :], blk(CTR, XX, i)[:, rows], m1, True, False, tx, ybw, tct)
                        last = mm(PS[rows, yb, :], blk(CTI, XX, i)[:, rows], m3, False, True, ty)
                        for x in (m1, m2, m3, m4):
                            stm.give(x, last)
                        yield
                    (y, w0_), (z, w1_) = stm.take(), stm.take()
                    t = stt(y, su[:, i, :], s5d[:, i:i + 1], ps(yb), MUL, ADD, last, w0_, K)
                    banks.give(yb, t)
                    t = tt(dve, z, y, y, MUL, t, w1_)
                    t = ts(dve, z, z, 0.044715, 1.0, MUL, ADD, t)
                    t = tt(dve, z, z, y, MUL, t)
                    t = af(z, z, ACT.Sigmoid, t, scale=2.0 * 0.7978845608028654)
                    yield
                    t = tt(dve, su[:, i, :], y, z, MUL, t)
                    stm.give(y, t)
                    stm.give(z, t)
                    tok["ys", i] = [t]
                    yield

            GA, gaw = tmps.take()
            got = {}

            def evac_ga(m, s, b, t):
                got["ga"] = af(GA[0:16, :], ps(b, 512, slice(0, 16)), ACT.Copy, t, gaw)
                banks.give(b, got["ga"])

            linear(WI, [(1024, 16, [(0, 0, 16)])], [8], hrhs, (0,), evac_ga)
            linear(WI, tiles(3096, 4), [8], hrhs, (0,), evac_to(su, 0, "su"))
            side.append(s5())

            def log_sigmoid(rows, z, tmp, t):
                t1_ = stt(tmp[rows, :], z[rows, :], -1.0, z[rows, :], MUL, MAX, t)
                t1_ = af(tmp[rows, :], tmp[rows, :], ACT.Exp, t1_, scale=-1.0)
                t1_ = af(tmp[rows, :], tmp[rows, :], ACT.Ln, t1_, K, bias=onec[rows, :])
                return stt(z[rows, :], z[rows, :], 0.0, tmp[rows, :], MIN, SUB, t1_)

            tcum = []
            allr = slice(0, 128)
            for m in range(2):
                b, bw = banks.take()
                last = mm(ps(b), A2[:, m * 128:(m + 1) * 128], GA[0:16, :], True, True, bw, got["ga"], tm)
                (z, w0_), (y, w1_) = tmps.take(), tmps.take()
                t = ts(dve, z, ps(b), glab[:, m:m + 1], None, ADD, None, last, w0_, K)
                banks.give(b, t)
                t = log_sigmoid(allr, z, y, [t, w1_])
                t = scan(dve, cum[:, m * 512:(m + 1) * 512], onec.to_broadcast([128, 512]), z, 0.0, MUL, ADD, t, fence)
                tcum.append(t)
                tmps.give(z, t)
                tmps.give(y, t)
            tmps.give(GA, last)

            def evac_gqk(m, s, b, t):
                t = af(gqk[:, m, :], ps(b), ACT.Copy, t, fence, scale=0.125 if m < 2 else 1.0)
                banks.give(b, t)
                tok["gqk", m] = [t]

            linear(WI, tiles(0, 4), [8], hrhs, (0,), evac_gqk)
            for c in range(2):
                tk = {}
                token_major(WI, 512 + 256 * c, 256, lambda j: gv[:, j, 256 * c:256 * c + 256], tk, 4, fence)
                for j in range(4):
                    tok.setdefault(("gv", j), []).extend(tk[j])
            tqk = [tok["gqk", m] for m in range(4)]
            GQ, GK = (arena(o_, 1024) for o_ in (0, 1024))
            tsd = fill(dve, SD.rearrange("p a n -> p (a n)"), 0.0, fence)
            tso = {}

            def gla_level(lv, h):
                if h:
                    nb = 512 // h
                    L = lambda x: x.rearrange("p (b c) -> p b c", c=2 * h)
                    ref = L(cum)[:, :, h - 1:h].to_broadcast([128, nb, h])
                    t1_ = tt(dve, L(EX)[:, :, 0:h], ref, L(cum)[:, :, 0:h], SUB, tcum, got.get("ex"))
                    t2_ = tt(dve, L(EX)[:, :, h:2 * h], L(cum)[:, :, h:2 * h], ref, SUB)
                    t = af(EX, EX, ACT.Exp, t1_, t2_, scale=1.0 / 16)
                    qk, w = QKL.take()
                    t1_ = tt(dve, L(qk)[:, :, 0:h], L(EX)[:, :, 0:h], L(GK)[:, :, 0:h], MUL, t, w, tqk)
                    t2_ = tt(pool, L(qk)[:, :, h:2 * h], L(EX)[:, :, h:2 * h], L(GQ)[:, :, h:2 * h], MUL, t, w, tqk)
                    got["ex"] = [t1_, t2_]
                    lt, rt, tw = qk, qk, [t1_, t2_]
                else:
                    lt, rt, tw = GK, GQ, tqk
                for hd in range(4):
                    r, o_ = slice(64 * (hd % 2), 64 * (hd % 2) + 64), 512 * (hd // 2)
                    b, bw = banks.take()
                    if h >= 128:
                        jobs = [(0, 256, 256, 128), (1, 256, 256, 384)] if h == 256 else [(0, 128, 128, 0), (2, 384, 128, 640)]
                        for n_, (s, t0, n, so) in enumerate(jobs):
                            last = mm(PS[:, b, n_ * 256:n_ * 256 + n], lt[r, o_ + s * 128:o_ + s * 128 + 128],
                                      rt[r, o_ + t0:o_ + t0 + n], True, True, bw, tw)
                        for n_, (s, t0, n, so) in enumerate(jobs):
                            t = af(SO[:, hd, so:so + n], PS[:, b, n_ * 256:n_ * 256 + n], ACT.Copy, last, fence)
                        tso.setdefault(hd, []).append(t)
                    else:
                        for s in range(4):
                            x = o_ + s * 128
                            last = mm(PS[:, b, s * 128:s * 128 + 128], lt[r, x:x + 128], rt[r, x:x + 128], True, True, bw, tw)
                        mk = MSK[:, lv, :].unsqueeze(1).to_broadcast([128, 4, 128])
                        sd = SD[:, hd, :].rearrange("p (a n) -> p a n", n=128)
                        t = cpred(dve, sd, mk, ps(b).rearrange("p (a n) -> p a n", n=128), last, tsd, tm, tso.get(("d", hd)))
                        tso["d", hd] = [t]
                    banks.give(b, t)
                if h:
                    QKL.give(qk, last)

            for h in (256, 128):
                gla_level(None, h)
                step()
            for lv, h in enumerate((64, 32, 16, 8, 4, 2, 1, 0)):
                gla_level(lv, h)
                step()
            gfence = P.fence()
            OG = gqk
            tog = {}
            for hd in range(4):
                b, bw = banks.take()
                w = [tso[hd], tso["d", hd], bw]
                for s in range(4):
                    v = gv[:, s, hd * 128:hd * 128 + 128]
                    w.append(tok["gv", s])
                    last = mm(PS[:, b, s * 128:s * 128 + 128], v, SD[:, hd, s * 128:s * 128 + 128], s == 0, s == 3, w)
                    if s < 3:
                        so = (0, 384, 640)[s]
                        last = mm(PS[:, b, (s + 1) * 128:512], v, SO[:, hd, so:so + 384 - 128 * s], False, False)
                t = af(OG[:, hd, :], ps(b), ACT.Copy, last, gfence)
                banks.give(b, t)
                x, xw = tmps.take()
                t2_ = af(x, OG[:, hd, :], ACT.Square, t, xw)
                b, bw = banks.take()
                last = mm(ps(b), mat["ones"], x, True, True, bw, t2_)
                tmps.give(x, last)
                tr_ = rstd(b, 512, 1.0 / 128, last, 0)
                t = stt(OG[:, hd, :], OG[:, hd, :], glanw[:, hd:hd + 1], STAT[0], MUL, MUL, tr_, t)
                statt[0] = [t]
                tog[hd] = [t]
                step()
            gfence = P.fence()

            tz = fill(dve, mqk[:, :, 0:3], 0.0, fence)
            linear(WI, tiles(1552, 4), [8], hrhs, (0,), evac_to(mqk, 0, "mqk", off=3))
            for c in range(2):
                tk = {}
                token_major(WI, 2064 + 256 * c, 256, lambda j: mv[:, j, 256 * c:256 * c + 256], tk, 4, fence)
                for j in range(4):
                    tok.setdefault(("mv", j), []).extend(tk[j])
            slot, v, vl, t = weights([(WI[:, 2576:2580], 0), (WI[:, 2580:2584], 32)], 8, 36, zero=True)
            gb, bw = banks.take()
            for k in range(8):
                last = mm3(ps(gb, 512, slice(0, 36)), (v[:, k, :], vl[:, k, :]), hseg(k, 0), k == 0, k == 7, t, bw, ht[k, 0])
            release(slot, last)
            (x0, f0), (x1, f1), (x2, f2) = (tmps.take() for _ in range(3))
            ri, rf = slice(0, 4), slice(32, 36)
            ti = ts(dve, x0[ri, :], ps(gb, 512, ri), ib[ri, :], None, ADD, None, last, f0, K)
            tf = ts(dve, x1[rf, :], ps(gb, 512, rf), ib[rf, :], None, ADD, None, f1)
            banks.give(gb, tf)
            t = log_sigmoid(rf, x1, x2, [tf, f2])
            t = cp(dve, x2[ri, :], x1[rf, :], t)
            BB = EX[ri, 0:512]
            MM = EX[ri, 512:1024]
            t = scan(dve, BB, onec[ri, :].to_broadcast([4, 512]), x2[ri, :], 0.0, MUL, ADD, t, gfence)
            ta = tt(dve, x0[ri, :], x0[ri, :], BB, SUB, t, ti)
            tM = scan(dve, MM, x0[ri, :], x0[ri, :], 0.0, MAX, MAX, ta)
            t = tt(dve, x2[ri, :], BB, MM, ADD, tM)
            t = ts(dve, x2[ri, :], x2[ri, :], -85.0, None, MAX, None, t)
            tem = af(x2[ri, :], x2[ri, :], ACT.Exp, t, scale=-1.0)
            b, bw = banks.take()
            for s in range(4):
                last = tr(PS[:, b, 4 * s:4 * s + 4], x0[ri, s * 128:(s + 1) * 128], 4, ta, bw)
            acol = col("acol", 16)
            tac = cp(dve, acol, PS[:, b, 0:16], last)
            banks.give(b, tac)
            tmps.give(x1, tac)
            tmps.give(x0, tac)
            mc = arena(14352, 2, 512)
            mcs = [mc[:, 0, :], mc[:, 1, :], arena(16400, 512), arena(16912, 512)]
            ex = arena(17424, 512)
            tmc = {}
            for m in range(4):
                y = mcs[m]
                t = ts(dve, y, mqk[:, m, 0:512], cw[:, 0, m:m + 1], cb[:, m:m + 1], MUL, ADD, tok["mqk", m], tz, gfence, K)
                for j in range(1, 4):
                    t = stt(y, mqk[:, m, j:j + 512], cw[:, j, m:m + 1], y, MUL, ADD, t)
                t = af(ex, y, ACT.Sigmoid, t, got.get("exw"))
                t = stt(y, y, 1.0 if m < 2 else 0.125, ex, MUL, MUL, t)
                got["exw"] = [t]
                tmc[m] = [t]
                step()
            OM = arena(4096, 4, 512)
            PM = SD
            tom = {}
            tpm = gfence
            pfence = P.fence()
            for hd in range(4):
                r = slice(64 * (hd % 2), 64 * (hd % 2) + 64)
                q_, k_ = mcs[hd // 2], mcs[2 + hd // 2]
                bM, bw = banks.take()
                lM = mm(ps(bM), sel(hd), MM, True, True, bw, tM, tm)
                tp = {}
                for s in range(4):
                    n = 512 - 128 * s
                    d = PM[:, s, 128 * s:512]
                    t = ts(dve, d, PS[:, bM, 128 * s:512], acol[:, 4 * s + hd:4 * s + hd + 1], 0.0, SUB, MAX, lM, tac, tpm)
                    if s == 3:
                        banks.give(bM, t)
                    t = af(d, d, ACT.Exp, t, scale=-1.0)
                    b, bw = banks.take()
                    last = mm(PS[:, b, 0:n], k_[r, s * 128:(s + 1) * 128], q_[r, 128 * s:512], True, True, bw,
                              tmc[hd // 2], tmc[2 + hd // 2])
                    t = tt(dve, d, PS[:, b, 0:n], d, MUL, last, t)
                    banks.give(b, t)
                    t = tt(pool, d[:, 0:128], d[:, 0:128], mat["causal"], MUL, t)
                    tp[s] = [t]
                bd, w0_ = banks.take()
                bn, w1_ = banks.take()
                for s in range(4):
                    ld = mm(PS[:, bd, 128 * s:512], mat["ones"], PM[:, s, 128 * s:512], s == 0, s == 3, w0_, tp[s])
                for s in range(4):
                    ln = mm(PS[:, bn, 128 * s:512], mv[:, s, hd * 128:hd * 128 + 128], PM[:, s, 128 * s:512],
                            s == 0, s == 3, w1_, tok["mv", s])
                be, w2_ = banks.take()
                le = mm(ps(be), sel(hd), x2[ri, :], True, True, w2_, tem)
                tpm = [ln]
                x, xw = tmps.take()
                t = af(x, ps(be), ACT.Copy, le, xw)
                banks.give(be, t)
                t = stt(x, ps(bd), -1.0, x, MUL, MAX, t, ld)
                t = tt(dve, x, ps(bd), x, MAX, t)
                banks.give(bd, t)
                t = recip(dve, x, x, t)
                t = tt(dve, OM[:, hd, :], ps(bn), x, MUL, t, ln, pfence)
                banks.give(bn, t)
                tmps.give(x, t)
                tom[hd] = [t]
                step()
            tmps.give(x2, le)
            mfence = P.fence()

            OGb, OMb = arena2(10256, 4, 512), arena2(12304, 4, 512)

            def evac_gr(m, s, b, t):
                x, w = tmps.take()
                t = af(x, ps(b), ACT.Sigmoid, t, w)
                if m < 4:
                    t = tt(dve, x, ps(b), x, MUL, t)
                banks.give(b, t)
                o_, oo, tq = (OG, OGb, tog) if m < 4 else (OM, OMb, tom)
                t = tt(pool, x, o_[:, m % 4, :], x, MUL, t, tq[m % 4])
                t = split(x, both(oo, slice(None), m % 4), t, mfence, q=pool)
                tmps.give(x, t)
                tq[m % 4] = [t]

            linear(WI, tiles(1040, 4), [8], hrhs, (0,), evac_gr)
            linear(WI, [(c, n, [(m + 4, o_, M) for m, o_, M in ms]) for c, n, ms in tiles(2584, 4)], [8], hrhs, (0,), evac_gr)
            YS = arena2(2048, 4, 512)
            tys = {}

            def evac_glu(m, s, b, t):
                x, w = tmps.take()
                t = af(x, ps(b), ACT.Sigmoid, t, w, K, bias=glub[:, m:m + 1])
                banks.give(b, t)
                t = tt(dve, x, su[:, m, :], x, MUL, t)
                t = split(x, both(YS, slice(None), m), t, mfence)
                tmps.give(x, t)
                tys[m] = [t]

            part = [arena(14352 + m * 512, 512) for m in range(8)]
            MG = [arena2(14352 + m * 512, 512) for m in range(8)]
            tmg = {}
            sgs = {}
            proj = [(a["proj_gla_2"][0], OGb, tog), (a["proj_ml_2"][0], OMb, tom), (a["proj_s5_2"][0], YS, tys)]
            tmps = Ring([arena(o_ + i * 512, 512) for o_ in (6160, 18448) for i in range(4)], P.fence())

            def branch(bi, mp):
                W, Yb, ty = proj[bi]

                def evac_z(m, s, b, t):
                    x, w = tmps.take()
                    t = af(x, ps(b), ACT.Sigmoid, t, w, K, bias=bgb[:, bi * 8 + m:bi * 8 + m + 1])
                    banks.give(b, t)
                    sgs[m] = (x, t)

                def evac_p(m, s, b, t):
                    x, tx = sgs[m]
                    if bi == 0:
                        t = tt(dve, part[m], ps(b), x, MUL, t, tx, mfence)
                        banks.give(b, t)
                        tmps.give(x, t)
                        tmg[m] = [t]
                        return
                    t = tt(dve, x, ps(b), x, MUL, t, tx)
                    banks.give(b, t)
                    if bi == 1:
                        t = tt(pool, part[m], part[m], x, ADD, t, tmg[m])
                        tmps.give(x, t)
                        tmg[m] = [t]
                        return
                    t = tt(pool, x, part[m], x, ADD, t, tmg[m])
                    tmg[m] = [split(x, [MG[m][:, i, :] for i in range(2)], t, q=pool)]
                    tmps.give(x, tmg[m])

                linear(WI, [(3608 + bi * 1024 + mp * 256, 256, [(2 * mp + j, 128 * j, 128) for j in range(2)])], [8],
                       hrhs, (0,), evac_z)
                linear(W, [(mp * 256, 256, [(2 * mp + j, 128 * j, 128) for j in range(2)])], [4],
                       lambda k, s: (both(Yb, slice(None), k), ty[k]), (0,), evac_p)

            for bi in range(2):
                for mp in range(4):
                    branch(bi, mp)
            drain()
            linear(a["s5_glu_w_2"][0], tiles(0, 4), [4], lambda k, s: (su[:, k, :], tok["ys", k]), (0,), evac_glu, whole=True)
            for mp in range(4):
                branch(2, mp)
            mfence = P.fence()
            Y = arena(0, 8, 512)
            yt = {}

            def evac_y(f, s, b, t):
                t = af(Y[:, f, :], ps(b), ACT.Copy, t, mfence)
                banks.give(b, t)
                yt[f] = [t]

            linear(a["w_out_2"][0], tiles(0, 8), [8], lambda k, s: ([MG[k][:, i, :] for i in range(2)], tmg[k]), (0,), evac_y)
            add_rms(Y, yt, nrm["post1_w_2"], 0, tmps)
        if "ffn" in parts:
            fence = P.fence()
            hid = arena2(0, 22, 512)
            Y = arena(11264, 8, 512)
            tmps = tmp_ring(15360, 8, fence)
            rms_mod(nrm["pre2_w_2"], 1, tmps, pe.last())
            hidt = {}
            W1 = a["ffn_w_in_2"][0]
            for m in range(22):
                slot, v, vl, t = weights([(W1[:, m * 128:(m + 1) * 128], 0), (W1[:, 2816 + m * 128:2944 + m * 128], 128)], 8, 256)
                bs = []
                for half in range(2):
                    b, bw = banks.take()
                    c = slice(half * 128, half * 128 + 128)
                    for k in range(8):
                        last = mm3(ps(b), (v[:, k, c], vl[:, k, c]), hseg(k, 0), k == 0, k == 7, bw, t, ht[k, 0])
                    bs.append((b, last))
                release(slot, last)
                (b0, l0), (b1, l1) = bs
                tmp, tw = tmps.take()
                t = af(tmp, ps(b0), ACT.Sigmoid, l0, tw)
                t = tt(dve, tmp, ps(b0), tmp, MUL, t)
                banks.give(b0, t)
                t = tt(dve, tmp, ps(b1), tmp, MUL, t, l1)
                banks.give(b1, t)
                t = split(tmp, both(hid, slice(None), m), t, fence, q=pool)
                tmps.give(tmp, t)
                hidt[m] = [t]
            yt = {}

            def evac_y(f, s, b, t):
                t = af(Y[:, f, :], ps(b), ACT.Copy, t, fence)
                banks.give(b, t)
                yt[f] = [t]
            linear(a["ffn_w_out_2"][0], tiles(0, 8), [8, 8, 6], lambda k, s: (both(hid, slice(None), k), hidt[k]), (0,), evac_y)
            add_rms(Y, yt, nrm["post2_w_2"], 1, tmps)

        s_out = P.sem("s_out")
        fence = P.fence()
        xo = arena(0, 4, 1024)
        for j in range(4):
            tk = []
            for half in range(2):
                b, bw = banks.take()
                for i in range(4):
                    f = half * 4 + i
                    last = tr(PS[:, b, i * 128:(i + 1) * 128], X[:, f, j * 128:(j + 1) * 128], 128, xt[f, 0], bw)
                dst = xo[:, j, half * 512:(half + 1) * 512]
                if half:
                    t = cp(dve, dst, ps(b), last, fence)
                else:
                    t = af(dst, ps(b), ACT.Copy, last, fence)
                banks.give(b, t)
                tk.append(t)
            tout = P.dma(sp, s_out, out[0, j * 128:(j + 1) * 128, :], xo[:, j, :], tk)
        ends = [tout]
        with nc.Block() as block:
            P.emit(block, ends)


INS = ["x", "c", "ctx", "c_ctx", "w_ada", "b_ada", "ln_g", "ln_b", "mlp_w1", "mlp_w2", "gqa_w_qkv", "gqa_q_norm",
       "gqa_k_norm", "gqa_w_o", "mla_w_in", "mla_q_norm", "mla_kv_norm", "mla_w_uq", "mla_w_ukv", "mla_w_o", "c_2",
       "ada_w_2", "ada_b_2", "pre1_w_2", "post1_w_2", "pre2_w_2", "post2_w_2", "w_in_2", "gla_a2_2", "gla_a_b_2",
       "gla_norm_w_2", "ml_conv_w_2", "ml_conv_b_2", "ml_i_b_2", "ml_f_b_2", "s5_lam_re_2", "s5_lam_im_2",
       "s5_log_step_2", "s5_b_re_2", "s5_b_im_2", "s5_c_re_2", "s5_c_im_2", "s5_d_2", "s5_glu_w_2", "s5_glu_b_2",
       "proj_gla_2", "proj_ml_2", "proj_s5_2", "branch_gate_b_2", "w_out_2", "ffn_w_in_2", "ffn_w_out_2"]


def kernel(**inputs):
    import concourse.bacc as bacc
    from concourse.bass_utils import run_bass_kernel_spmd

    nc = bacc.Bacc("TRN2", target_bir_lowering=False, num_devices=1)
    arrays, aps = {}, {}
    given = {n: np.ascontiguousarray(inputs[n]) for n in INS}
    given.update(constants())
    for name, v in given.items():
        arrays["in_" + name] = v
        aps[name] = nc.dram_tensor("in_" + name, v.shape, mybir.dt.from_np(v.dtype), kind="ExternalInput").ap()
    out = nc.dram_tensor("out_0", (1, 512, 1024), F32, kind="ExternalOutput").ap()
    build(nc, aps, out)
    r = run_bass_kernel_spmd(nc, [arrays], core_ids=[0])
    return r.results[0]["out_0"]
```
